# Optimizing a Trainium2 kernel written in Bass

```python
import math
import jax
import jax.numpy as jnp
from jax import lax
import numpy as np

D_MODEL = 2048
BATCH = 1
SEQ = 256
DEPTH = 1

MEM_LEN = 256
EPS = 1e-6
DN_HEADS = 8
DN_DK = 128
DN_DV = 128
DN_CONV = 4
DN_CHUNK = 64
SWA_HEADS = 8
SWA_KV_HEADS = 2
SWA_DH = 64
WINDOW = 128
SB_HEADS = 4
SB_DH = 128
SB_BLOCK = 128
X_HEADS = 4
X_DH = 128
D_FF = 4096
FFN_CONV = 3
N_BRANCH = 3

DN_QK_WIDTH = DN_HEADS * DN_DK
DN_WIDTH = DN_HEADS * DN_DV
SWA_WIDTH = SWA_HEADS * SWA_DH
SWA_KV_WIDTH = SWA_KV_HEADS * SWA_DH
SB_WIDTH = SB_HEADS * SB_DH
X_WIDTH = X_HEADS * X_DH
IN_SIZES = (2 * DN_QK_WIDTH + DN_WIDTH, DN_WIDTH, DN_HEADS, DN_HEADS, SWA_WIDTH, 2 * SWA_KV_WIDTH, 3 * SB_WIDTH, N_BRANCH * D_MODEL)
IN_COLS = sum(IN_SIZES)


def rmsnorm(x, g):
    xf = x.astype(jnp.float32)
    y = xf * lax.rsqrt(jnp.mean(xf * xf, axis=-1, keepdims=True) + EPS)
    return (y * g.astype(jnp.float32)).astype(x.dtype)

def l2norm(x):
    xf = x.astype(jnp.float32)
    return xf * lax.rsqrt(jnp.sum(xf * xf, axis=-1, keepdims=True) + EPS)

def causal_dwconv(x, w):
    width = w.shape[0]
    seq = x.shape[1]
    xp = jnp.pad(x, ((0, 0), (width - 1, 0), (0, 0)))
    out = xp[:, 0:seq] * w[0]
    for i in range(1, width):
        out = out + xp[:, i:i + seq] * w[i]
    return out

def split_cols(t, sizes):
    offsets = [int(o) for o in np.cumsum(sizes)[:-1]]
    return jnp.split(t, offsets, axis=-1)

def alibi_slopes(n):
    return jnp.exp2(-8.0 * (jnp.arange(n, dtype=jnp.float32) + 1.0) / n)

def gated_delta_rule(q, k, v, g, beta):
    bsz, seq, heads, dk = q.shape
    dv = v.shape[-1]
    c = DN_CHUNK
    n = seq // c
    f32 = jnp.float32

    def chunks(t):
        return t.astype(f32).reshape(bsz, n, c, heads, -1).transpose(0, 1, 3, 2, 4)

    qc = chunks(q) * (dk ** -0.5)
    kc = chunks(k)
    vc = chunks(v)
    gc = jnp.cumsum(g.astype(f32).reshape(bsz, n, c, heads).transpose(0, 1, 3, 2), axis=-1)
    bc = beta.astype(f32).reshape(bsz, n, c, heads).transpose(0, 1, 3, 2)[..., None]
    causal = jnp.tril(jnp.ones((c, c), dtype=bool))
    strict = jnp.tril(jnp.ones((c, c), dtype=bool), -1)
    diff = gc[..., :, None] - gc[..., None, :]
    decay = jnp.where(causal, jnp.exp(jnp.where(causal, diff, 0.0)), 0.0)
    kb = kc * bc
    kk = jnp.einsum('bnhid,bnhjd->bnhij', kb, kc) * decay
    t_mat = jnp.eye(c, dtype=f32) + jnp.where(strict, kk, 0.0)
    u = lax.linalg.triangular_solve(t_mat, vc * bc, left_side=True, lower=True, unit_diagonal=True)
    w = lax.linalg.triangular_solve(t_mat, kb * jnp.exp(gc)[..., None], left_side=True, lower=True, unit_diagonal=True)
    qk = jnp.einsum('bnhid,bnhjd->bnhij', qc, kc) * decay
    q_dec = qc * jnp.exp(gc)[..., None]
    k_dec = kc * jnp.exp(gc[..., -1:] - gc)[..., None]
    g_last = jnp.exp(gc[..., -1])

    def step(state, xs):
        qk_n, qd_n, kd_n, u_n, w_n, gl_n = xs
        v_new = u_n - jnp.einsum('bhcd,bhde->bhce', w_n, state)
        o = jnp.einsum('bhcd,bhde->bhce', qd_n, state) + jnp.einsum('bhij,bhje->bhie', qk_n, v_new)
        state = state * gl_n[..., None, None] + jnp.einsum('bhcd,bhce->bhde', kd_n, v_new)
        return state, o

    xs = tuple(jnp.moveaxis(t, 1, 0) for t in (qk, q_dec, k_dec, u, w, g_last))
    state0 = jnp.zeros((bsz, heads, dk, dv), f32)
    _, o = lax.scan(step, state0, xs)
    return o.transpose(1, 0, 3, 2, 4).reshape(bsz, seq, heads, dv)

def sliding_window_gqa(q, k, v, sinks):
    bsz, seq = q.shape[:2]
    n = seq // WINDOW
    grp = SWA_HEADS // SWA_KV_HEADS
    qb = q.reshape(bsz, n, WINDOW, SWA_KV_HEADS, grp, SWA_DH)

    def band(t):
        tb = t.reshape(bsz, n, WINDOW, SWA_KV_HEADS, SWA_DH)
        prev = jnp.pad(tb, ((0, 0), (1, 0), (0, 0), (0, 0), (0, 0)))[:, :-1]
        return jnp.concatenate([prev, tb], axis=2)

    kb = band(k)
    vb = band(v)
    s = jnp.einsum('bnqhgd,bnkhd->bnhgqk', qb, kb).astype(jnp.float32) * (SWA_DH ** -0.5)
    qi = jnp.arange(WINDOW)[:, None]
    kj = jnp.arange(2 * WINDOW)[None, :]
    dist = qi + WINDOW - kj
    blk = jnp.arange(n)[:, None, None]
    valid = (dist >= 0) & (dist < WINDOW) & (blk * WINDOW + kj - WINDOW >= 0)
    slopes = alibi_slopes(SWA_HEADS).reshape(SWA_KV_HEADS, grp)[:, :, None, None]
    s = s - slopes * dist.astype(jnp.float32)
    s = jnp.where(valid[None, :, None, None], s, -jnp.inf)
    sink = sinks.astype(jnp.float32).reshape(SWA_KV_HEADS, grp)[:, :, None, None]
    m = jnp.maximum(jnp.max(s, axis=-1, keepdims=True), sink)
    p = jnp.exp(s - m)
    p = p / (jnp.sum(p, axis=-1, keepdims=True) + jnp.exp(sink - m))
    o = jnp.einsum('bnhgqk,bnkhd->bnqhgd', p.astype(vb.dtype), vb)
    return o.reshape(bsz, seq, SWA_WIDTH)

def stick_breaking_attention(q, k, v):
    bsz, seq, heads, dh = q.shape
    n = seq // SB_BLOCK
    f32 = jnp.float32
    tri_incl = jnp.tril(jnp.ones((SB_BLOCK, SB_BLOCK), f32))
    tri_blocks = jnp.tril(jnp.ones((n, n), f32), -1)
    scale = dh ** -0.5
    outs = []
    for i in range(n):
        nk = i + 1
        length = nk * SB_BLOCK
        q_blk = q[:, i * SB_BLOCK:(i + 1) * SB_BLOCK]
        k_blk = k[:, :length]
        v_blk = v[:, :length]
        z = jnp.einsum('bqhd,bshd->bhqs', q_blk, k_blk).astype(f32) * scale
        qpos = i * SB_BLOCK + jnp.arange(SB_BLOCK)
        valid = jnp.arange(length)[None, :] < qpos[:, None]
        zm = jnp.where(valid, z, -jnp.inf)
        l = jax.nn.log_sigmoid(-zm).reshape(bsz, heads, SB_BLOCK, nk, SB_BLOCK)
        rev_in = jnp.einsum('bhqnj,js->bhqns', l, tri_incl)
        after = jnp.einsum('bhqm,mn->bhqn', jnp.sum(l, axis=-1), tri_blocks[:nk, :nk])
        rev = (rev_in + after[..., None]).reshape(bsz, heads, SB_BLOCK, length)
        a = jnp.exp(zm + rev)
        outs.append(jnp.einsum('bhqs,bshd->bqhd', a.astype(v.dtype), v_blk))
    o = jnp.concatenate(outs, axis=1)
    return o.reshape(bsz, seq, heads * dh)

def hybrid_mixer(xn, w_in, dn_conv, dn_a_log, dn_dt_bias, dn_norm, swa_sinks, w_br_dn, w_br_swa, w_br_sb, w_o):
    bsz, seq, _ = xn.shape
    proj = xn @ w_in
    dn_qkv, dn_z, dn_a, dn_b, swa_q, swa_kv, sb_qkv, gates = split_cols(proj, IN_SIZES)
    dn_qkv = jax.nn.silu(causal_dwconv(dn_qkv, dn_conv))
    q, k, v = split_cols(dn_qkv, (DN_QK_WIDTH, DN_QK_WIDTH, DN_WIDTH))
    q = l2norm(q.reshape(bsz, seq, DN_HEADS, DN_DK))
    k = l2norm(k.reshape(bsz, seq, DN_HEADS, DN_DK))
    v = v.reshape(bsz, seq, DN_HEADS, DN_DV)
    g = -jnp.exp(dn_a_log.astype(jnp.float32)) * jax.nn.softplus(dn_a.astype(jnp.float32) + dn_dt_bias.astype(jnp.float32))
    beta = jax.nn.sigmoid(dn_b.astype(jnp.float32))
    o_dn = gated_delta_rule(q, k, v, g, beta)
    o_dn = rmsnorm(o_dn, dn_norm) * jax.nn.silu(dn_z.reshape(bsz, seq, DN_HEADS, DN_DV).astype(jnp.float32))
    y_dn = o_dn.reshape(bsz, seq, DN_WIDTH).astype(xn.dtype)
    swa_k, swa_v = split_cols(swa_kv, (SWA_KV_WIDTH, SWA_KV_WIDTH))
    y_swa = sliding_window_gqa(swa_q.reshape(bsz, seq, SWA_HEADS, SWA_DH), swa_k.reshape(bsz, seq, SWA_KV_HEADS, SWA_DH), swa_v.reshape(bsz, seq, SWA_KV_HEADS, SWA_DH), swa_sinks)
    sb_q, sb_k, sb_v = split_cols(sb_qkv, (SB_WIDTH, SB_WIDTH, SB_WIDTH))
    y_sb = stick_breaking_attention(sb_q.reshape(bsz, seq, SB_HEADS, SB_DH), sb_k.reshape(bsz, seq, SB_HEADS, SB_DH), sb_v.reshape(bsz, seq, SB_HEADS, SB_DH))
    gate = jax.nn.sigmoid(gates).reshape(bsz, seq, N_BRANCH, D_MODEL)
    merged = gate[:, :, 0] * (y_dn @ w_br_dn) + gate[:, :, 1] * (y_swa @ w_br_swa) + gate[:, :, 2] * (y_sb @ w_br_sb)
    return merged @ w_o

def memory_cross_attention(hn, mem_n, w_xq, w_xkv, w_xo):
    bsz, seq, _ = hn.shape
    q = (hn @ w_xq).reshape(bsz, seq, X_HEADS, X_DH)
    kv = (mem_n @ w_xkv).reshape(bsz, mem_n.shape[1], 2, X_HEADS, X_DH)
    s = jnp.einsum('bqhd,bmhd->bhqm', q, kv[:, :, 0]).astype(jnp.float32) * (X_DH ** -0.5)
    p = jax.nn.softmax(s, axis=-1)
    o = jnp.einsum('bhqm,bmhd->bqhd', p.astype(kv.dtype), kv[:, :, 1])
    return o.reshape(bsz, seq, X_WIDTH) @ w_xo

def conv_ffn(hn, w_up, ffn_conv, w_down):
    up = causal_dwconv(hn @ w_up, ffn_conv)
    gate, val = jnp.split(up, 2, axis=-1)
    return (jax.nn.silu(gate) * val) @ w_down

def first_inputs(seed: int = 0) -> dict:
    key = jax.random.key(seed)
    ks = jax.random.split(key, 24)
    f32 = jnp.float32

    def dense(k, shape, fan_in):
        return jax.random.normal(k, shape, f32) * (fan_in ** -0.5)

    def gain(k, shape):
        return 1.0 + 0.02 * jax.random.normal(k, shape, f32)

    dt = jnp.exp(jax.random.uniform(ks[6], (DEPTH, DN_HEADS), f32, minval=math.log(1e-3), maxval=math.log(0.1)))
    return {
        'x': jax.random.normal(ks[0], (BATCH, SEQ, D_MODEL), f32),
        'mem': jax.random.normal(ks[1], (BATCH, MEM_LEN, D_MODEL), f32),
        'norm_mix': gain(ks[2], (DEPTH, D_MODEL)),
        'w_in': dense(ks[3], (DEPTH, D_MODEL, IN_COLS), D_MODEL),
        'dn_conv': dense(ks[4], (DEPTH, DN_CONV, 2 * DN_QK_WIDTH + DN_WIDTH), DN_CONV),
        'dn_a_log': jnp.log(jax.random.uniform(ks[5], (DEPTH, DN_HEADS), f32, minval=1.0, maxval=16.0)),
        'dn_dt_bias': dt + jnp.log(-jnp.expm1(-dt)),
        'dn_norm': gain(ks[7], (DEPTH, DN_DV)),
        'swa_sinks': 0.5 * jax.random.normal(ks[8], (DEPTH, SWA_HEADS), f32),
        'w_br_dn': dense(ks[9], (DEPTH, DN_WIDTH, D_MODEL), DN_WIDTH),
        'w_br_swa': dense(ks[10], (DEPTH, SWA_WIDTH, D_MODEL), SWA_WIDTH),
        'w_br_sb': dense(ks[11], (DEPTH, SB_WIDTH, D_MODEL), SB_WIDTH),
        'w_o': dense(ks[12], (DEPTH, D_MODEL, D_MODEL), D_MODEL),
        'norm_xattn': gain(ks[13], (DEPTH, D_MODEL)),
        'norm_mem': gain(ks[14], (DEPTH, D_MODEL)),
        'w_xq': dense(ks[15], (DEPTH, D_MODEL, X_WIDTH), D_MODEL),
        'w_xkv': dense(ks[16], (DEPTH, D_MODEL, 2 * X_WIDTH), D_MODEL),
        'w_xo': dense(ks[17], (DEPTH, X_WIDTH, D_MODEL), X_WIDTH),
        'norm_ffn': gain(ks[18], (DEPTH, D_MODEL)),
        'w_up': dense(ks[19], (DEPTH, D_MODEL, 2 * D_FF), D_MODEL),
        'ffn_conv': dense(ks[20], (DEPTH, FFN_CONV, 2 * D_FF), FFN_CONV),
        'w_down': dense(ks[21], (DEPTH, D_FF, D_MODEL), D_FF),
        'norm_final': gain(ks[22], (D_MODEL,)),
    }

def first_block(x, mem, norm_mix, w_in, dn_conv, dn_a_log, dn_dt_bias, dn_norm, swa_sinks, w_br_dn, w_br_swa, w_br_sb, w_o, norm_xattn, norm_mem, w_xq, w_xkv, w_xo, norm_ffn, w_up, ffn_conv, w_down, norm_final):
    h = x
    for l in range(DEPTH):
        h = h + hybrid_mixer(rmsnorm(h, norm_mix[l]), w_in[l], dn_conv[l], dn_a_log[l], dn_dt_bias[l], dn_norm[l], swa_sinks[l], w_br_dn[l], w_br_swa[l], w_br_sb[l], w_o[l])
        h = h + memory_cross_attention(rmsnorm(h, norm_xattn[l]), rmsnorm(mem, norm_mem[l]), w_xq[l], w_xkv[l], w_xo[l])
        h = h + conv_ffn(rmsnorm(h, norm_ffn[l]), w_up[l], ffn_conv[l], w_down[l])
    return rmsnorm(h, norm_final)


N_MIXERS = 3
N_HEADS = 16
HEAD_DIM = D_MODEL // N_HEADS
D_FF_2 = 4 * D_MODEL
CONV_WIDTH = 31
MOBA_BLOCK = 256
MOBA_TOPK = 3
MOBA_Q_CHUNK = 16
FOX_Q_BLOCK = 128
NORM_EPS = 1e-6
NEG_INF = -1e30
LAYER_MIXERS = tuple(i % N_MIXERS for i in range(DEPTH))
N_CONV = LAYER_MIXERS.count(0)
N_MOBA = LAYER_MIXERS.count(1)
N_FOX = LAYER_MIXERS.count(2)


def _rms_norm(x, g):
    xf = x.astype(jnp.float32)
    y = xf * lax.rsqrt(jnp.mean(xf * xf, axis=-1, keepdims=True) + NORM_EPS)
    return (y * g.astype(jnp.float32)).astype(x.dtype)

def _layer_norm(x, g, b):
    xf = x.astype(jnp.float32)
    mu = jnp.mean(xf, axis=-1, keepdims=True)
    var = jnp.mean(jnp.square(xf - mu), axis=-1, keepdims=True)
    y = (xf - mu) * lax.rsqrt(var + NORM_EPS)
    return (y * g.astype(jnp.float32) + b.astype(jnp.float32)).astype(x.dtype)

def _split_heads(z):
    b, s, _ = z.shape
    return z.reshape(b, s, N_HEADS, HEAD_DIM).transpose(0, 2, 1, 3)

def _merge_blocks(o):
    nb, b, h, q, d = o.shape
    return o.transpose(1, 0, 3, 2, 4).reshape(b, nb * q, h * d)

def _conv_mixer(h, w_in, b_in, dw_w, dw_b, ln_g, ln_b, w_out, b_out):
    u = h @ w_in + b_in
    a, gt = jnp.split(u, 2, axis=-1)
    u = a * jax.nn.sigmoid(gt)
    u = lax.conv_general_dilated(
        u, dw_w[:, None, :].astype(u.dtype), window_strides=(1,),
        padding=[(CONV_WIDTH - 1, 0)],
        dimension_numbers=('NWC', 'WIO', 'NWC'),
        feature_group_count=D_MODEL) + dw_b
    u = jax.nn.silu(_layer_norm(u, ln_g, ln_b))
    return u @ w_out + b_out

def _moba_mixer(h, w_qkv, q_g, k_g, w_o):
    b, s, _ = h.shape
    q, k, v = jnp.split(h @ w_qkv, 3, axis=-1)
    q = _rms_norm(_split_heads(q), q_g)
    k = _rms_norm(_split_heads(k), k_g)
    v = _split_heads(v)
    nb = -(-s // MOBA_BLOCK)
    pad = nb * MOBA_BLOCK - s
    kp = jnp.pad(k, ((0, 0), (0, 0), (0, pad), (0, 0)))
    vp = jnp.pad(v, ((0, 0), (0, 0), (0, pad), (0, 0)))
    kb = kp.reshape(b, N_HEADS, nb, MOBA_BLOCK, HEAD_DIM)
    vb = vp.reshape(b, N_HEADS, nb, MOBA_BLOCK, HEAD_DIM)
    kmean = jnp.mean(kb, axis=3)
    topk = min(MOBA_TOPK, nb)
    scale = HEAD_DIM ** -0.5
    n_chunks = s // MOBA_Q_CHUNK
    qc = q.reshape(b, N_HEADS, n_chunks, MOBA_Q_CHUNK, HEAD_DIM).transpose(2, 0, 1, 3, 4)
    blk_ids = jnp.arange(nb)
    gather = jax.vmap(jax.vmap(lambda kk, ii: kk[ii]))

    def chunk(args):
        ci, qi = args
        t0 = ci * MOBA_Q_CHUNK
        cur = t0 // MOBA_BLOCK
        gate = jnp.einsum('bhqd,bhnd->bhqn', qi, kmean).astype(jnp.float32)
        gate = jnp.where(blk_ids < cur, gate, NEG_INF)
        _, sel = lax.top_k(gate, topk)
        valid = sel < cur
        k_sel = gather(kb, sel)
        v_sel = gather(vb, sel)
        s_sel = jnp.einsum('bhqd,bhqkjd->bhqkj', qi, k_sel).astype(jnp.float32) * scale
        s_sel = jnp.where(valid[..., None], s_sel, NEG_INF)
        s_sel = s_sel.reshape(b, N_HEADS, MOBA_Q_CHUNK, topk * MOBA_BLOCK)
        k_own = lax.dynamic_slice_in_dim(kp, cur * MOBA_BLOCK, MOBA_BLOCK, axis=2)
        v_own = lax.dynamic_slice_in_dim(vp, cur * MOBA_BLOCK, MOBA_BLOCK, axis=2)
        s_own = jnp.einsum('bhqd,bhjd->bhqj', qi, k_own).astype(jnp.float32) * scale
        t_pos = t0 + jnp.arange(MOBA_Q_CHUNK)
        s_pos = cur * MOBA_BLOCK + jnp.arange(MOBA_BLOCK)
        s_own = jnp.where(s_pos[None, :] <= t_pos[:, None], s_own, NEG_INF)
        p = jax.nn.softmax(jnp.concatenate([s_sel, s_own], axis=-1), axis=-1)
        p_sel = p[..., :topk * MOBA_BLOCK].reshape(b, N_HEADS, MOBA_Q_CHUNK, topk, MOBA_BLOCK)
        p_own = p[..., topk * MOBA_BLOCK:]
        o = jnp.einsum('bhqkj,bhqkjd->bhqd', p_sel.astype(v.dtype), v_sel)
        o = o + jnp.einsum('bhqj,bhjd->bhqd', p_own.astype(v.dtype), v_own)
        return o

    o = lax.map(chunk, (jnp.arange(n_chunks), qc))
    return _merge_blocks(o) @ w_o

def _fox_mixer(h, w_in, b_f, q_g, k_g, w_o):
    b, s, _ = h.shape
    proj = h @ w_in
    d = D_MODEL
    q = _rms_norm(_split_heads(proj[..., :d]), q_g)
    k = _rms_norm(_split_heads(proj[..., d:2 * d]), k_g)
    v = _split_heads(proj[..., 2 * d:3 * d])
    g_out = proj[..., 3 * d:4 * d]
    log_f = jax.nn.log_sigmoid((proj[..., 4 * d:] + b_f).astype(jnp.float32))
    cum = jnp.cumsum(log_f, axis=1).transpose(0, 2, 1)
    scale = HEAD_DIM ** -0.5
    nqb = s // FOX_Q_BLOCK
    qb = q.reshape(b, N_HEADS, nqb, FOX_Q_BLOCK, HEAD_DIM).transpose(2, 0, 1, 3, 4)
    cq = cum.reshape(b, N_HEADS, nqb, FOX_Q_BLOCK).transpose(2, 0, 1, 3)
    s_pos = jnp.arange(s)

    def block(args):
        bi, qi, ci = args
        t_pos = bi * FOX_Q_BLOCK + jnp.arange(FOX_Q_BLOCK)
        logits = jnp.einsum('bhqd,bhsd->bhqs', qi, k).astype(jnp.float32) * scale
        logits = logits + (ci[..., :, None] - cum[:, :, None, :])
        logits = jnp.where(s_pos[None, :] <= t_pos[:, None], logits, NEG_INF)
        p = jax.nn.softmax(logits, axis=-1)
        return jnp.einsum('bhqs,bhsd->bhqd', p.astype(v.dtype), v)

    o = _merge_blocks(lax.map(block, (jnp.arange(nqb), qb, cq)))
    o = o * jax.nn.sigmoid(g_out)
    return o @ w_o

def _normal(k, shape, scale):
    return scale * jax.random.normal(k, shape, jnp.float32)

def second_inputs(seed: int = 0) -> dict:
    key = jax.random.key(seed)
    ks = iter(jax.random.split(key, 32))
    d = D_MODEL
    sd = d ** -0.5
    return {
        'x': _normal(next(ks), (BATCH, SEQ, d), 1.0),
        'c': _normal(next(ks), (BATCH, d), 1.0),
        'norm1_g': 1.0 + _normal(next(ks), (DEPTH, d), 0.02),
        'norm2_g': 1.0 + _normal(next(ks), (DEPTH, d), 0.02),
        'mod_w': _normal(next(ks), (DEPTH, d, 6 * d), 0.5 * sd),
        'mod_b': _normal(next(ks), (DEPTH, 6 * d), 0.02),
        'mlp_w1': _normal(next(ks), (DEPTH, d, D_FF_2), sd),
        'mlp_w2': _normal(next(ks), (DEPTH, D_FF_2, d), D_FF_2 ** -0.5),
        'conv_w_in': _normal(next(ks), (N_CONV, d, 2 * d), sd),
        'conv_b_in': _normal(next(ks), (N_CONV, 2 * d), 0.02),
        'conv_dw_w': _normal(next(ks), (N_CONV, CONV_WIDTH, d), CONV_WIDTH ** -0.5),
        'conv_dw_b': _normal(next(ks), (N_CONV, d), 0.02),
        'conv_ln_g': 1.0 + _normal(next(ks), (N_CONV, d), 0.02),
        'conv_ln_b': _normal(next(ks), (N_CONV, d), 0.02),
        'conv_w_out': _normal(next(ks), (N_CONV, d, d), sd),
        'conv_b_out': _normal(next(ks), (N_CONV, d), 0.02),
        'moba_w_qkv': _normal(next(ks), (N_MOBA, d, 3 * d), sd),
        'moba_q_g': 1.0 + _normal(next(ks), (N_MOBA, HEAD_DIM), 0.02),
        'moba_k_g': 1.0 + _normal(next(ks), (N_MOBA, HEAD_DIM), 0.02),
        'moba_w_o': _normal(next(ks), (N_MOBA, d, d), sd),
        'fox_w_in': _normal(next(ks), (N_FOX, d, 4 * d + N_HEADS), sd),
        'fox_b_f': 2.0 + _normal(next(ks), (N_FOX, N_HEADS), 0.5),
        'fox_q_g': 1.0 + _normal(next(ks), (N_FOX, HEAD_DIM), 0.02),
        'fox_k_g': 1.0 + _normal(next(ks), (N_FOX, HEAD_DIM), 0.02),
        'fox_w_o': _normal(next(ks), (N_FOX, d, d), sd),
    }

def second_block(x, c, norm1_g, norm2_g, mod_w, mod_b, mlp_w1, mlp_w2,
              conv_w_in, conv_b_in, conv_dw_w, conv_dw_b, conv_ln_g, conv_ln_b,
              conv_w_out, conv_b_out, moba_w_qkv, moba_q_g, moba_k_g, moba_w_o,
              fox_w_in, fox_b_f, fox_q_g, fox_k_g, fox_w_o):
    cond = jax.nn.silu(c)
    for i in range(DEPTH):
        kind = LAYER_MIXERS[i]
        j = i // N_MIXERS
        mod = cond @ mod_w[i] + mod_b[i]
        sh1, sc1, g1, sh2, sc2, g2 = jnp.split(mod, 6, axis=-1)
        h = _rms_norm(x, norm1_g[i]) * (1.0 + sc1[:, None, :]) + sh1[:, None, :]
        if kind == 0:
            y = _conv_mixer(h, conv_w_in[j], conv_b_in[j], conv_dw_w[j], conv_dw_b[j],
                            conv_ln_g[j], conv_ln_b[j], conv_w_out[j], conv_b_out[j])
        elif kind == 1:
            y = _moba_mixer(h, moba_w_qkv[j], moba_q_g[j], moba_k_g[j], moba_w_o[j])
        else:
            y = _fox_mixer(h, fox_w_in[j], fox_b_f[j], fox_q_g[j], fox_k_g[j], fox_w_o[j])
        x = x + (1.0 + g1[:, None, :]) * y
        h = _rms_norm(x, norm2_g[i]) * (1.0 + sc2[:, None, :]) + sh2[:, None, :]
        u = jnp.square(jax.nn.relu(h @ mlp_w1[i]))
        x = x + (1.0 + g2[:, None, :]) * (u @ mlp_w2[i])
    return x


def setup_inputs(seed=0):
    out = dict(first_inputs(seed))
    for name, value in second_inputs(seed + 1).items():
        if name != "x":
            out[name + "_2"] = value
    return out


def reference(
    x, mem, norm_mix, w_in, dn_conv, dn_a_log, dn_dt_bias, dn_norm, swa_sinks, w_br_dn,
    w_br_swa, w_br_sb, w_o, norm_xattn, norm_mem, w_xq, w_xkv, w_xo, norm_ffn, w_up, ffn_conv,
    w_down, norm_final, c_2, norm1_g_2, norm2_g_2, mod_w_2, mod_b_2, mlp_w1_2, mlp_w2_2,
    conv_w_in_2, conv_b_in_2, conv_dw_w_2, conv_dw_b_2, conv_ln_g_2, conv_ln_b_2, conv_w_out_2,
    conv_b_out_2, moba_w_qkv_2, moba_q_g_2, moba_k_g_2, moba_w_o_2, fox_w_in_2, fox_b_f_2,
    fox_q_g_2, fox_k_g_2, fox_w_o_2,
):
    x = first_block(
        x, mem, norm_mix, w_in, dn_conv, dn_a_log, dn_dt_bias, dn_norm, swa_sinks, w_br_dn,
        w_br_swa, w_br_sb, w_o, norm_xattn, norm_mem, w_xq, w_xkv, w_xo, norm_ffn, w_up,
        ffn_conv, w_down, norm_final,
    )
    return second_block(
        x, c_2, norm1_g_2, norm2_g_2, mod_w_2, mod_b_2, mlp_w1_2, mlp_w2_2, conv_w_in_2,
        conv_b_in_2, conv_dw_w_2, conv_dw_b_2, conv_ln_g_2, conv_ln_b_2, conv_w_out_2,
        conv_b_out_2, moba_w_qkv_2, moba_q_g_2, moba_k_g_2, moba_w_o_2, fox_w_in_2, fox_b_f_2,
        fox_q_g_2, fox_k_g_2, fox_w_o_2,
    )


_drawn_inputs = setup_inputs


def setup_inputs(seed=0):
    import zlib

    import numpy as np

    out = dict(_drawn_inputs(seed))
    spreads = {}
    factors = {'norm_mix': 3.388,
     'dn_norm': 8.0,
     'swa_sinks': 29.897,
     'norm_xattn': 8.0,
     'norm_mem': 8.0,
     'norm_ffn': 3.843,
     'norm1_g_2': 4.765,
     'norm2_g_2': 3.184,
     'conv_b_in_2': 4.668,
     'conv_ln_g_2': 4.112,
     'conv_ln_b_2': 4.734,
     'conv_b_out_2': 3.021,
     'conv_dw_b_2': 7.448}
    for name, (base, spread) in spreads.items():
        noise = np.random.default_rng([zlib.crc32(name.encode()), seed]).standard_normal(out[name].shape)
        drawn = base * np.exp(spread * noise) if base else spread * noise
        out[name] = jnp.asarray(drawn.astype(out[name].dtype))
    for name, factor in factors.items():
        out[name] = (out[name] * factor).astype(out[name].dtype)
    return out
```

```python
from contextlib import ExitStack, contextmanager

import concourse.bass as bass
from concourse import mybir

ALU = mybir.AluOpType
ACT = mybir.ActivationFunctionType
F32 = mybir.dt.float32
F32R = mybir.dt.float32r
AX_X = mybir.AxisListType.X

P = 128
T = 256
TT = T // P
D = 2048
KT = D // P
CH = 512
UK = 2
SLOTS = 4
EPS = 1e-6
FAR = 1e30

DN_H, DK = 8, 128
DN_W = DN_H * DK
DN_TAPS = 4
WIN_H, WIN_DH = 8, 64
ST_H, ST_DH = 4, 128
X_H, X_DH = 4, 128
FF = 4096
FF_TAPS = 3
MLP = 8192
TAPS = 31
TAP_U = 2
PE_TAPS = 8
PE_TAPS_LAST = 12
GROUP = 4
LEVELS = 7

C_Z = 3 * DN_W
C_AB = C_Z + DN_W
C_WQ = C_AB + 2 * DN_H
C_WKV = C_WQ + WIN_H * WIN_DH
C_ST = C_WKV + 4 * WIN_DH
C_GATE = C_ST + 3 * ST_H * ST_DH

MOD = 6 * D
MOD_W = 1536
MOD_B = MOD_W // P
MOD_G = MOD // MOD_W


def at(base, *loops):
    for register, step in loops:
        base = register * step + base
    return base


class Plan:

    def __init__(self):
        self.unit = self.chunk = 0
        self.start = {}

    def lay(self, name, sizes, times=1):
        self.start[name] = (self.unit, self.chunk, sizes)
        self.unit += times * sum(sizes)
        self.chunk += times * len(sizes)

    def spot(self, name, c, *loops):
        u, ch, sizes = self.start[name]
        return Spot(u + sum(sizes[:c]), ch + c, sizes[c], loops)


class Spot:

    def __init__(self, unit, chunk, size, loops):
        self.unit, self.chunk, self.size = unit, chunk, size
        self.loops = loops
        self.pair = chunk % 2

    def slot(self, k):
        return (self.unit + k) % SLOTS

    def units(self, k):
        return at(self.unit + k, *[(r, u) for r, u, _ in self.loops])

    def loads(self, k):
        return at(16 * ((self.unit + k) // SLOTS + 1), *[(r, 16 * u // SLOTS) for r, u, _ in self.loops])

    def reads(self, more=0):
        return at(self.chunk // 2 + more, *[(r, c // 2) for r, _, c in self.loops])


class Own:

    def __init__(self, eng, sem):
        self.eng, self.sem, self.n, self.loops = eng, sem, 0, []

    def step(self, ins):
        ins.then_inc(self.sem, 1)
        self.n += 1
        return self.n

    def wait(self, n=None):
        self.eng.wait_ge(self.sem, at(self.n if n is None else n, *self.loops))

    @contextmanager
    def loop(self, times, steps):
        with self.eng.Fori(0, times) as i:
            start = self.n
            self.loops.append((i, steps))
            yield i
            assert self.n - start == steps, (self.n - start, steps)
            self.loops.pop()
        self.n = start + times * steps


def build_program(nc, x, mem, w_in, dn_conv, dn_a_log, dn_dt_bias, dn_norm, norm_mix, swa_sinks, w_br_dn, w_br_swa,
                  w_br_sb, w_o, norm_xattn, norm_mem, w_xq, w_xkv, w_xo, norm_ffn, w_up, ffn_conv, w_down,
                  norm_final, c_2, norm1_g_2, norm2_g_2, mod_w_2, mod_b_2, mlp_w1_2, mlp_w2_2, conv_w_in_2,
                  conv_b_in_2, conv_dw_w_2, conv_dw_b_2, conv_ln_g_2, conv_ln_b_2, conv_w_out_2, conv_b_out_2, out):
    plan = Plan()
    plan.lay("ab", [2])
    plan.lay("delta", [8] * 8)
    plan.lay("window", [8, 4])
    plan.lay("stick", [8, 8, 8])
    plan.lay("merge", [8, 8, 8, 4, 2, 2], 4)
    plan.lay("mix_out", [8, 8], 2)
    plan.lay("mem_kv", [8, 8])
    plan.lay("cross_q", [8])
    plan.lay("cross_out", [2, 2, 2, 2])
    plan.lay("ffn_up", [8, 8], 4)
    plan.lay("ffn_down", [8, 8], 2)
    FFN_U, FFN_C = 96, 12
    plan.unit += FFN_U
    plan.chunk += FFN_C
    plan.lay("conv_in", [8, 8], 4)
    plan.lay("conv_out", [8, 8], 2)
    plan.lay("mlp_up", [8, 8], 2)
    plan.lay("mlp_down", [8, 8], 2)
    MLP_Q = MLP // D
    MLP_U, MLP_C = 64, 8
    plan.unit += (MLP_Q - 1) * MLP_U
    plan.chunk += (MLP_Q - 1) * MLP_C
    spot = plan.spot
    ADDED = 4 + 4 * MLP_Q

    def rows(a):
        return a.rearrange("(r p) -> r p", p=P)

    dn_rows = dn_conv[0].rearrange("i (b p) -> (i b) p", p=P)
    ffn_rows = ffn_conv[0].rearrange("i (b p) -> (i b) p", p=P)
    dw_rows = conv_dw_w_2[0].rearrange("i (b p) -> (i b) p", p=P)
    groups = [
        [("mix", rows(norm_mix[0])), ("xattn", rows(norm_xattn[0])), ("mem", rows(norm_mem[0])),
         ("ffn", rows(norm_ffn[0])), ("n1", rows(norm1_g_2[0])), ("n2", rows(norm2_g_2[0]))],
        [("mod_b", rows(mod_b_2[0]))],
        [("b_in", rows(conv_b_in_2[0])), ("dw_b", rows(conv_dw_b_2[0])), ("ln_g", rows(conv_ln_g_2[0])),
         ("ln_b", rows(conv_ln_b_2[0])), ("c", rows(c_2[0])), ("dn_norm", rows(dn_norm[0]))],
        [("dn_conv", dn_rows)],
        [("ffn_conv", ffn_rows[0:96])], [("ffn_conv1", ffn_rows[96:192])],
        [("dw", dw_rows[0:124])], [("dw1", dw_rows[124:248])], [("dw2", dw_rows[248:372])], [("dw3", dw_rows[372:496])],
    ]
    col, n_par = {}, 0
    for group in groups:
        for name, a in group:
            col[name] = n_par
            n_par += a.shape[0]
    n_par_loads = sum(map(len, groups))

    with ExitStack() as ctx:
        def sb(name, shape, dt=F32, scope=ctx):
            return scope.enter_context(nc.sbuf_tensor(name, shape, dt))

        def sem(name):
            return ctx.enter_context(nc.semaphore(name))

        h = sb("h", [P, TT, D])
        raw = sb("raw", [P, SLOTS, UK * CH])
        w_hi = sb("w_hi", [P, SLOTS, UK * CH], F32R)
        w_lo = sb("w_lo", [P, SLOTS, UK * CH], F32R)
        x_hi = sb("x_hi", [P, KT, T], F32R)
        x_lo = sb("x_lo", [P, KT, T], F32R)
        with ExitStack() as s:
            mem_in = sb("mem_in", [P, TT, D], scope=s)
            mem_x = sb("mem_x", [P, TT, D], scope=s)
        y_hi = sb("y_hi", [P, KT, T], F32R)
        y_lo = sb("y_lo", [P, KT, T], F32R)
        ident = sb("ident", [P, P])
        ones = sb("ones", [P, P])
        later = sb("later", [P, P])
        causal = sb("causal", [P, P])
        strict = sb("strict", [P, P])
        level = sb("level", [P, LEVELS + 1, P])
        twice = sb("twice", [P, 2, P])
        dist = sb("dist", [P, 2 * P])
        par = sb("par", [P, n_par])
        cond = sb("cond", [P, KT])
        mod = sb("mod", [P, 6 * KT])
        eff = sb("eff", [P, KT])
        sinks = sb("sinks", [P, WIN_H])
        dt_b = sb("dt_b", [2 * DN_H, 1])
        a_log = sb("a_log", [2 * DN_H, 1])
        a_exp = sb("a_exp", [2 * DN_H, 1])
        gb_nat = sb("gb_nat", [P, 64])
        g_sum = sb("g_sum", [2 * DN_H, T])
        beta = sb("beta", [2 * DN_H, T])
        stat = sb("stat", [P, 8, 8])
        eps_col = sb("eps_col", [P, 1])

        with ExitStack() as s:
            norm_x = sb("norm_x", [P, TT, D], scope=s)
            norm_v = sb("norm_v", [P, 2, 2, T], scope=s)
            rows_in = sb("rows_in", [P, len(groups), P], scope=s)
        with ExitStack() as s:
            pad3 = sb("pad3", [P, GROUP, DN_TAPS - 1 + T], scope=s)
            qkv = sb("qkv", [P, 3 * GROUP, T], scope=s)
            z_t = sb("z_t", [P, GROUP, T], scope=s)
            work = sb("work", [P, 4, 1024], scope=s)
            beta_b = sb("beta_b", [P, GROUP, T], scope=s)
            decay = sb("decay", [P, 2, GROUP * P], scope=s)
            low_t = sb("low_t", [P, 2, GROUP * P], scope=s)
            qk_t = sb("qk_t", [P, 2, GROUP * P], scope=s)
            v_nat = sb("v_nat", [P, 2, GROUP * P], scope=s)
            k_nat = sb("k_nat", [P, 2, GROUP * P], scope=s)
            q_dec = sb("q_dec", [P, GROUP, P], scope=s)
        with ExitStack() as s:
            win_q = sb("win_q", [P, 4, T], scope=s)
            win_k = sb("win_k", [P, T], scope=s)
            win_k2 = sb("win_k2", [P, 2, T], scope=s)
            win_v = sb("win_v", [P, TT, P], scope=s)
            soft_s = sb("soft_s", [P, 8, T], scope=s)
            soft_pt = sb("soft_pt", [P, 16, P], scope=s)
            heads_o = sb("heads_o", [P, 4, T], scope=s)
            st_q = sb("st_q", [P, ST_H, T], scope=s)
            st_k = sb("st_k", [P, ST_H, T], scope=s)
            st_v = sb("st_v", [P, TT, CH], scope=s)
            st_z = sb("st_z", [P, ST_H, 3 * P], scope=s)
            st_e = sb("st_e", [P, ST_H, 3 * P], scope=s)
        mods = ctx.enter_context(ExitStack())
        mod_raw = sb("mod_raw", [P, 2, MOD_W], scope=mods)
        mod_acc = sb("mod_acc", [P, MOD_W], scope=mods)
        with ExitStack() as s:
            m_hi = sb("m_hi", [P, KT, T], F32R, scope=s)
            m_lo = sb("m_lo", [P, KT, T], F32R, scope=s)
            gate = sb("gate", [P, 3, 4, T], scope=s)
        with ExitStack() as s:
            cr_k = sb("cr_k", [P, X_H, T], scope=s)
            cr_v = sb("cr_v", [P, TT, CH], scope=s)
            with ExitStack() as s1:
                norm_x2 = sb("norm_x2", [P, TT, D], scope=s1)
                norm_v2 = sb("norm_v2", [P, 2, 2, T], scope=s1)
            with ExitStack() as s1:
                cr_q = sb("cr_q", [P, X_H, T], scope=s1)
                cr_s = sb("cr_s", [P, 8, T], scope=s1)
                cr_pt = sb("cr_pt", [P, 16, P], scope=s1)
                cr_o = sb("cr_o", [P, X_H, T], scope=s1)
            with ExitStack() as s1:
                pad2 = sb("pad2", [P, 4, FF_TAPS - 1 + T], scope=s1)
                ff_g = sb("ff_g", [P, 4, T], scope=s1)
                ff_v = sb("ff_v", [P, 4, T], scope=s1)
        mods.close()
        with ExitStack() as s:
            gate_b = sb("gate_b", [P, 2, D], scope=s)
            bias_b = sb("bias_b", [P, D], scope=s)
            with ExitStack() as s1:
                diag = sb("diag", [P, KT, P], scope=s1)
                norm_x3 = sb("norm_x3", [P, TT, D], scope=s1)
                norm_v3 = sb("norm_v3", [P, 2, 2, T], scope=s1)
                final_b = sb("final_b", [P, D], scope=s1)
            with ExitStack() as s1:
                cv_a = sb("cv_a", [P, 4, T], scope=s1)
                cv_g = sb("cv_g", [P, 4, T], scope=s1)
                pad30 = sb("pad30", [P, 4, TAPS - 1 + T], scope=s1)
                cv = sb("cv", [P, KT, T], scope=s1)
                ln_m = sb("ln_m", [P, 2, T], scope=s1)
                tap_diag = sb("tap_diag", [P, 2, TAP_U, P], scope=s1)
            with ExitStack() as s1:
                ml_r = sb("ml_r", [P, 4, T], scope=s1)
                ml_t = sb("ml_t", [P, TT, CH], scope=s1)

        mem_v = gate[:, 0, :, :].rearrange("p (a b) t -> p a b t", b=2)

        sums = ctx.enter_context(nc.psum_tensor("sums", [P, 2, 2, CH], F32))
        small = ctx.enter_context(nc.psum_tensor("small", [P, 4, CH], F32))

        const_made = sem("const_made")
        const_ready = sem("const_ready")
        par_loaded = sem("par_loaded")
        vec_loaded = sem("vec_loaded")
        x_loaded = sem("x_loaded")
        mem_loaded = sem("mem_loaded")
        wide_loaded = sem("wide_loaded")
        raw_loaded = [sem(f"raw_loaded{i}") for i in range(SLOTS)]
        hi_ready = sem("hi_ready")
        lo_ready = sem("lo_ready")
        unit_used = sem("unit_used")
        bank_read = [sem(f"bank_read{i}") for i in range(2)]
        act_own = sem("act_own")
        dve_own = sem("dve_own")
        eps_made = sem("eps_made")
        par_turned = sem("par_turned")
        par_kept = sem("par_kept")
        cond_made = sem("cond_made")
        norm_squared = sem("norm_squared")
        norm_mean = sem("norm_mean")
        norm_root = sem("norm_root")
        norm_scaled = sem("norm_scaled")
        norm_turned = sem("norm_turned")
        norm_gained = sem("norm_gained")
        norm_split = sem("norm_split")
        ab_abs = sem("ab_abs")
        ab_log = sem("ab_log")
        ab_sum = sem("ab_sum")
        ab_turned = sem("ab_turned")
        ab_kept = sem("ab_kept")
        tap_done = sem("tap_done")
        dn_square = sem("dn_square")
        dn_sumsq = sem("dn_sumsq")
        dn_rnorm = sem("dn_rnorm")
        dn_unit = sem("dn_unit")
        dn_rows_b = sem("dn_rows_b")
        dn_rows_kept = sem("dn_rows_kept")
        dn_diff = sem("dn_diff")
        dn_decay = sem("dn_decay")
        dn_kk = sem("dn_kk")
        dn_qk = sem("dn_qk")
        dn_low = sem("dn_low")
        dn_scores = sem("dn_scores")
        dn_turned = sem("dn_turned")
        dn_nat = sem("dn_nat")
        sv_join = sem("sv_join")
        sv_prod = sem("sv_prod")
        sv_kept = sem("sv_kept")
        sv_corr = sem("sv_corr")
        sv_done = sem("sv_done")
        dn_step = sem("dn_step")
        dn_step_kept = sem("dn_step_kept")
        dn_step_kept_v = sem("dn_step_kept_v")
        dn_out = sem("dn_out")
        dn_out_kept = sem("dn_out_kept")
        dn_out_sq = sem("dn_out_sq")
        dn_out_rms = sem("dn_out_rms")
        y_split = sem("y_split")
        win_twice = sem("win_twice")
        win_twice_kept = sem("win_twice_kept")
        soft_scores = sem("soft_scores")
        soft_max = sem("soft_max")
        soft_exp = sem("soft_exp")
        soft_prob = sem("soft_prob")
        soft_turned = sem("soft_turned")
        soft_kept = sem("soft_kept")
        heads_out = sem("heads_out")
        heads_kept = sem("heads_kept")
        st_scores = sem("st_scores")
        st_masked = sem("st_masked")
        st_abs = sem("st_abs")
        st_log = sem("st_log")
        st_cost = sem("st_cost")
        st_summed = sem("st_summed")
        st_arg = sem("st_arg")
        st_weight = sem("st_weight")
        merged = sem("merged")
        h_added = sem("h_added")
        silu_done = sem("silu_done")
        ff_split = sem("ff_split")
        mod_loaded = [sem(f"mod_loaded{i}") for i in range(2)]
        mod_used = sem("mod_used")
        mod_clear = sem("mod_clear")
        mod_summed = sem("mod_summed")
        mod_kept = sem("mod_kept")
        final_ready = sem("final_ready")
        diag_made = sem("diag_made")
        diag_summed = sem("diag_summed")
        diag_kept = sem("diag_kept")
        glu_done = sem("glu_done")
        cv_tap = sem("cv_tap")
        cv_diag = sem("cv_diag")
        cv_diag_used = sem("cv_diag_used")
        cv_added = sem("cv_added")
        ln_sum = sem("ln_sum")
        ln_mean = sem("ln_mean")
        ln_centred = sem("ln_centred")
        ln_square = sem("ln_square")
        ln_var = sem("ln_var")
        ln_rstd = sem("ln_rstd")
        ln_normed = sem("ln_normed")
        ln_silu = sem("ln_silu")
        cv_split = sem("cv_split")
        ml_split = sem("ml_split")
        out_stored = sem("out_stored")

        block = ctx.enter_context(nc.Block())

        def parm(name, c, n=1):
            return par[:, col[name] + c:col[name] + c + n]

        def parm_at(name, c, n=1):
            return par[:, bass.ds(c + col[name], n)]

        def unit_src(w, row, column, width):
            n = UK * CH // width
            r = slice(row, row + n * P) if isinstance(row, int) else bass.ds(row, n * P)
            c = slice(column, column + width) if isinstance(column, int) else bass.ds(column, width)
            return w[r, c].rearrange("(t p) n -> p t n", p=P)

        def load_chunk(sp, s, w, row, column, width=CH):
            n = UK * CH // width
            for k in range(s.size):
                src = unit_src(w, row + k * n * P, column, width)
                if s.unit + k >= SLOTS:
                    sp.wait_ge(lo_ready, s.units(k + 1 - SLOTS))
                sp.dma_start(raw[:, s.slot(k), :].rearrange("p (t n) -> p t n", n=width),
                             src).then_inc(raw_loaded[s.slot(k)], 16)

        def round_units(act, s, first, last):
            for k in range(first, last):
                act.wait_ge(raw_loaded[s.slot(k)], s.loads(k))
                if s.unit + k >= SLOTS:
                    act.wait_ge(unit_used, s.units(k + 1 - SLOTS))
                act.activation(w_hi[:, s.slot(k), :], raw[:, s.slot(k), :], ACT.Copy).then_inc(hi_ready, 1)

        def rest_units(dve, s, first, last, between=None, times=0):
            for k in range(first, last):
                dve.wait_ge(hi_ready, s.units(k + 1))
                dve.tensor_tensor(w_lo[:, s.slot(k), :], raw[:, s.slot(k), :], w_hi[:, s.slot(k), :].bitcast(F32),
                                  ALU.subtract).then_inc(lo_ready, 1)
                n, of = k - first, last - first
                for j in range(n * times // of, (n + 1) * times // of):
                    between(j)

        def ahead(s, last=False):
            return SLOTS, s.size + (0 if last else SLOTS)

        def multiply(pe, s, a_hi, a_lo, turned, width=CH, k0=0, before=None):
            if s.chunk >= 2:
                pe.wait_ge(bank_read[s.pair], s.reads())
            n = UK * CH // width
            for k in range(s.size):
                if before is not None:
                    before(k * n, (k + 1) * n)
                pe.wait_ge(lo_ready, s.units(k + 1))
                hi = w_hi[:, s.slot(k), :].rearrange("p (t n) -> p t n", n=width)
                lo = w_lo[:, s.slot(k), :].rearrange("p (t n) -> p t n", n=width)
                for t in range(n):
                    kt = k * n + t
                    end = kt == s.size * n - 1
                    for b in range(width // P) if turned else range(TT):
                        if turned:
                            o = sums[:, s.pair, b // 2, (b % 2) * T:(b % 2 + 1) * T]
                            wh, wl = hi[:, t, b * P:(b + 1) * P], lo[:, t, b * P:(b + 1) * P]
                            ah, al = a_hi[:, k0 + kt, :], a_lo[:, k0 + kt, :]
                            first = kt == 0 and b % 2 == 0
                            steps = [(wh, ah), (wh, al), (wl, ah)]
                        else:
                            o = sums[:, s.pair, b, 0:width]
                            ah, al = a_hi[:, k0 + kt, b * P:(b + 1) * P], a_lo[:, k0 + kt, b * P:(b + 1) * P]
                            first = kt == 0
                            steps = [(ah, hi[:, t, :]), (ah, lo[:, t, :]), (al, hi[:, t, :])]
                        for i, (l, r) in enumerate(steps):
                            mm = pe.matmul(o, l, r, start=first and i == 0, stop=end and i == 2, skip_group_check=True)
                mm.then_inc(unit_used, 1)

        def chunk_sums(s):
            return sums[:, s.pair, :, :].rearrange("p a n -> p (a n)").rearrange("p (b t) -> p b t", t=T)

        NG = KT // 2

        def rms_act(act, n, src, tmp):
            for t in range(TT):
                act.activation(tmp[:, t, :], src[:, t, :], ACT.Square,
                               accum_out=stat[:, 0, t:t + 1]).then_inc(norm_squared, 1)
            act.wait_ge(norm_mean, n + 1)
            act.activation(stat[:, 2, 0:TT], stat[:, 1, 0:TT], ACT.Sqrt).then_inc(norm_root, 1)

        def rms_dve(dve, own, n):
            dve.wait_ge(norm_squared, TT * (n + 1))
            dve.tensor_scalar(stat[:, 1, 0:TT], stat[:, 0, 0:TT], 1.0 / D, EPS, ALU.mult, ALU.add).then_inc(norm_mean, 1)
            dve.wait_ge(norm_root, n + 1)
            own.step(dve.reciprocal(stat[:, 3, 0:TT], stat[:, 2, 0:TT]))
            own.wait()

        def norm_act(act, n, v, gain, shift=None):
            for g in range(NG):
                act.wait_ge(norm_turned, NG * n + g + 1)
                if g >= 2:
                    act.wait_ge(norm_split, NG * n + g - 1)
                for j in range(2):
                    kt = 2 * g + j
                    ps = small[:, g % 4, j * T:(j + 1) * T]
                    if shift is None:
                        ins = act.activation(v[:, g % 2, j, :], ps, ACT.Copy, scale=gain(kt))
                    else:
                        ins = act.activation(v[:, g % 2, j, :], ps, ACT.Identity, scale=gain(kt), bias=shift(kt))
                ins.then_inc(norm_gained, 1)

        def norm_dve(dve, own, n, src, tmp, v, a_hi, a_lo):
            scale_rows(dve, src, tmp)
            split_channels(dve, own, n, v, a_hi, a_lo)

        def scale_rows(dve, src, tmp):
            for t in range(TT):
                dve.tensor_scalar(tmp[:, t, :], src[:, t, :], stat[:, 3, t:t + 1], None, ALU.mult).then_inc(norm_scaled, 1)

        def split_channels(dve, own, n, v, a_hi, a_lo):
            for g in range(NG):
                dve.wait_ge(norm_gained, NG * n + g + 1)
                own.step(dve.tensor_copy(a_hi[:, 2 * g:2 * g + 2, :], v[:, g % 2, :, :]))
                own.wait()
                dve.tensor_tensor(a_lo[:, 2 * g:2 * g + 2, :], v[:, g % 2, :, :],
                                  a_hi[:, 2 * g:2 * g + 2, :].bitcast(F32), ALU.subtract).then_inc(norm_split, 1)

        def turn_rows(pe, n, tmp, first, last):
            for g in range(first, last):
                if g >= 4:
                    pe.wait_ge(norm_gained, NG * n + g - 3)
                for j in range(2):
                    for t in range(TT):
                        ins = pe.transpose(small[:, g % 4, j * T + t * P:j * T + (t + 1) * P],
                                           tmp[:, t, (2 * g + j) * P:(2 * g + j + 1) * P], ident[:, :])
                ins.then_inc(norm_turned, 1)

        def norm_pe(pe, n, tmp, s, a_hi, a_lo, turned, width=CH):
            def before(tile, end):
                turn_rows(pe, n, tmp, min(tile // 2 + 4, NG), min(end // 2 + 4, NG))
                pe.wait_ge(norm_split, NG * n + end // 2)

            pe.wait_ge(norm_scaled, TT * (n + 1))
            turn_rows(pe, n, tmp, 0, 4)
            multiply(pe, s, a_hi, a_lo, turned, width, before=before)

        def win_scores(b, keys):
            at_ = (4 * (b % 2) + b // 2) * keys
            return small[:, at_ // CH, at_ % CH:at_ % CH + keys]

        def soft_dve(dve, own, n, s_t, keys, sink, pt):
            own.step(dve.tensor_reduce(stat[:, 4, :], s_t[:, :, 0:keys], AX_X, ALU.max))
            own.wait()
            if sink is not None:
                own.step(dve.tensor_tensor(stat[:, 4, :], stat[:, 4, :], sink[:, :], ALU.max))
                own.wait()
                own.step(dve.tensor_tensor(stat[:, 5, :], sink[:, :], stat[:, 4, :], ALU.subtract))
            dve.tensor_tensor(s_t[:, :, 0:keys], s_t[:, :, 0:keys],
                              stat[:, 4, :].unsqueeze(2).to_broadcast([P, 8, keys]), ALU.subtract).then_inc(soft_max, 1)
            dve.wait_ge(soft_exp, n + 1)
            own.wait()
            own.step(dve.tensor_reduce(stat[:, 7, :], s_t[:, :, 0:keys], AX_X, ALU.add))
            own.wait()
            if sink is not None:
                own.step(dve.tensor_tensor(stat[:, 7, :], stat[:, 7, :], stat[:, 6, :], ALU.add))
                own.wait()
            own.step(dve.reciprocal(stat[:, 7, :], stat[:, 7, :]))
            own.wait()
            dve.tensor_tensor(s_t[:, :, 0:keys], s_t[:, :, 0:keys],
                              stat[:, 7, :].unsqueeze(2).to_broadcast([P, 8, keys]), ALU.mult).then_inc(soft_prob, 1)

        def soft_act(act, n, s_t, keys, sink):
            act.wait_ge(soft_max, n + 1)
            if sink is not None:
                act.activation(stat[:, 6, :], stat[:, 5, :], ACT.Exp)
            act.activation(s_t[:, :, 0:keys], s_t[:, :, 0:keys], ACT.Exp).then_inc(soft_exp, 1)

        def soft_keep(act, keys, pt, base):
            tiles = 8 * keys // P
            for i in range(tiles // 4):
                act.wait_ge(soft_turned, base + i + 1)
                act.activation(pt[:, 4 * i:4 * i + 4, :].rearrange("p a b -> p (a b)"), small[:, i, :],
                               ACT.Copy).then_inc(soft_kept, 1)

        def soft_pe(pe, n, s_t, keys):
            pe.wait_ge(soft_prob, n + 1)
            tiles = keys // P
            for i in range(8 * tiles):
                ins = pe.transpose(small[:, i // 4, (i % 4) * P:(i % 4 + 1) * P],
                                   s_t[:, i // tiles, (i % tiles) * P:(i % tiles + 1) * P], ident[:, :])
                if i % 4 == 3:
                    ins.then_inc(soft_turned, 1)

        def heads_split(dve, own, n, o, first):
            dve.wait_ge(heads_kept, n)
            own.step(dve.tensor_copy(y_hi[:, first:first + 4, :], o))
            own.wait()
            dve.tensor_tensor(y_lo[:, first:first + 4, :], o, y_hi[:, first:first + 4, :].bitcast(F32),
                              ALU.subtract).then_inc(y_split, 1)

        def mod_unit(dve, m, kt, *loops):
            dve.wait_ge(mod_loaded[m % 2], at(16 * (m // 2 + 1), *[(r, 8 * n) for r, n in loops]))
            dve.wait_ge(mod_clear, at(m // 16 + 1, *[(r, n // 16) for r, n in loops]))
            if m > 0:
                dve.wait_ge(mod_used, at(m, *loops))
            c = cond[:, kt:kt + 1] if isinstance(kt, int) else cond[:, bass.ds(kt, 1)]
            dve.scalar_tensor_tensor(out=mod_acc[:, :], in0=mod_raw[:, m % 2, :], scalar=c, in1=mod_acc[:, :],
                                     op0=ALU.mult, op1=ALU.add).then_inc(mod_used, 1)

        def mod_sum(pe, used):
            pe.wait_ge(mod_used, used)
            for b in range(MOD_B):
                ins = pe.matmul(small[:, 3, b:b + 1], mod_acc[:, b * P:(b + 1) * P], ones[:, 0:1], start=True, stop=True)
            ins.then_inc(mod_summed, 1)

        def mod_keep(dve, q, summed):
            dve.wait_ge(mod_summed, summed)
            dve.tensor_tensor(mod[:, bass.ds(q * MOD_B, MOD_B)], small[:, 3, 0:MOD_B],
                              parm_at("mod_b", q * MOD_B, MOD_B), ALU.add).then_inc(mod_kept, 1)

        def added(eng, *chunks):
            for s in chunks:
                eng.wait_ge(bank_read[s.pair], s.reads(1))

        def multiply_kv(pe, s):
            pe.wait_ge(bank_read[s.pair], s.reads())
            width = 2 * P
            n = UK * CH // width
            for u in range(s.size):
                pe.wait_ge(lo_ready, s.units(u + 1))
                hi = w_hi[:, s.slot(u), :].rearrange("p (t n) -> p t n", n=width)
                lo = w_lo[:, s.slot(u), :].rearrange("p (t n) -> p t n", n=width)
                for t in range(n):
                    kt = u * n + t
                    end = kt == s.size * n - 1
                    wh, wl = hi[:, t, 0:P], lo[:, t, 0:P]
                    for i, (l, r) in enumerate(((wh, x_hi[:, kt, :]), (wh, x_lo[:, kt, :]), (wl, x_hi[:, kt, :]))):
                        pe.matmul(sums[:, s.pair, 0, 0:T], l, r, start=kt == 0 and i == 0, stop=end and i == 2,
                                  skip_group_check=True)
                    wh, wl = hi[:, t, P:], lo[:, t, P:]
                    for b in range(TT):
                        c = slice(b * P, (b + 1) * P)
                        for i, (l, r) in enumerate(((x_hi[:, kt, c], wh), (x_hi[:, kt, c], wl), (x_lo[:, kt, c], wh))):
                            mm = pe.matmul(sums[:, s.pair, 1, c], l, r, start=kt == 0 and b == 0 and i == 0,
                                           stop=end and i == 2, skip_group_check=True)
                mm.then_inc(unit_used, 1)

        def wide_dve(dve, n, blk):
            if n:
                dve.wait_ge(diag_summed, 4 * n)
            m = mod[:, blk * KT:(blk + 1) * KT].unsqueeze(2).to_broadcast([P, KT, P])
            dve.tensor_tensor(diag[:, :, :], ident[:, :].unsqueeze(1).to_broadcast([P, KT, P]), m,
                              ALU.mult).then_inc(diag_made, 1)

        def wide_pe(pe, n):
            pe.wait_ge(diag_made, n + 1)
            for j in range(4):
                if n:
                    pe.wait_ge(diag_kept, j + 1)
                pe.matmul(small[:, j, :], ones[:, :], diag[:, 4 * j:4 * j + 4, :].rearrange("p a b -> p (a b)"),
                          start=True, stop=True).then_inc(diag_summed, 1)

        def wide_act(act, n):
            for j in range(4):
                act.wait_ge(diag_summed, 4 * n + j + 1)
                act.activation(gate_b[:, n, j * CH:(j + 1) * CH], small[:, j, :], ACT.Copy, bias=1.0).then_inc(diag_kept, 1)

        HP = GROUP * P
        w_x, w_xt, w_off, w_prod = (work[:, i, :] for i in range(4))
        w_sq = work[:, 0:2, :].rearrange("p a n -> p (a n)")
        w_rn = work[:, 2:4, :].rearrange("p a n -> p (a n)")
        u0, nw = w_prod[:, 0:HP], w_prod[:, HP:]
        st1, vn1 = w_off[:, 0:HP], w_off[:, HP:]

        def two_banks(b):
            return small[:, b:b + 2, :].rearrange("p a n -> p (a n)")

        def by_head(t):
            return t.rearrange("p (b t) -> p b t", b=GROUP)

        def by_chunk(t):
            return t.rearrange("p b (c i) -> p c b i", c=TT)

        def split_chunk(t):
            return t.rearrange("p c (b i) -> p c b i", b=GROUP)

        def delta_silu(act, own, g):
            act.wait_ge(tap_done, 48 * (g + 1))
            own.step(act.activation(qkv[:, :, :], qkv[:, :, :], ACT.Silu))
            own.wait()
            act.activation(w_sq, qkv[:, 0:8, :].rearrange("p a t -> p (a t)"), ACT.Square).then_inc(dn_square, 1)

        def delta_act(act, own, g):
            act.wait_ge(dn_sumsq, g + 1)
            own.step(act.activation(w_rn, small[:, :, :].rearrange("p a n -> p (a n)"), ACT.Ln, bias=eps_col[:, 0:1]))
            own.wait()
            act.activation(w_rn, w_rn, ACT.Exp, scale=-0.5).then_inc(dn_rnorm, 1)
            act.wait_ge(dn_rows_b, g + 1)
            gcb = by_head(two_banks(0))
            act.activation(beta_b[:, :, :], by_head(two_banks(2)), ACT.Copy)
            act.activation(q_dec[:, :, :], gcb[:, :, P:], ACT.Exp)
            act.activation(stat[:, 4, 0:GROUP].unsqueeze(2), gcb[:, :, P - 1:P], ACT.Copy)
            act.activation(stat[:, 6, 0:GROUP], gb_nat[:, 16 + GROUP * g:16 + GROUP * (g + 1)],
                           ACT.Exp).then_inc(dn_rows_kept, 1)
            act.wait_ge(dn_diff, g + 1)
            act.activation(stat[:, 5, 0:GROUP], stat[:, 5, 0:GROUP], ACT.Exp)
            act.activation(decay[:, :, :], decay[:, :, :], ACT.Exp).then_inc(dn_decay, 1)
            with act.Fori(0, LEVELS) as l:
                for c in range(TT):
                    act.wait_ge(sv_prod, l * 2 + (14 * g + c + 1))
                    act.activation(w_prod[:, c * HP:(c + 1) * HP], small[:, c, :], ACT.Copy).then_inc(sv_kept, 1)
            act.wait_ge(dn_step, 4 * g + 1)
            act.activation(u0, small[:, 0, :], ACT.Copy).then_inc(dn_step_kept, 1)
            act.wait_ge(dn_step, 4 * g + 2)
            act.activation(nw, small[:, 1, :], ACT.Copy, scale=-1.0).then_inc(dn_step_kept, 1)
            act.wait_ge(dn_out, g + 1)
            own.step(act.activation(w_x, two_banks(0), ACT.Copy))
            own.wait()
            act.activation(w_xt, w_x, ACT.Square).then_inc(dn_out_sq, 1)
            act.wait_ge(dn_out_rms, g + 1)
            lt = low_t[:, :, :].rearrange("p a n -> p (a n)")
            own.step(act.activation(lt, two_banks(2), ACT.Ln, scale=1.0 / DK, bias=eps_col[:, 0:1]))
            own.wait()
            act.activation(lt, lt, ACT.Exp, scale=-0.5).then_inc(dn_rnorm, 1)

        def delta_dve(dve, own, g):
            dve.wait_ge(dn_rnorm, 2 * g + 1)
            qk = qkv[:, 0:8, :].rearrange("p a t -> p (a t)")
            dve.tensor_tensor(qk, qk, w_rn, ALU.mult).then_inc(dn_unit, 1)
            for x in (w_x, w_xt):
                dve.tensor_copy(x.rearrange("p (a b) -> p a b", b=P),
                                ident[:, :].unsqueeze(1).to_broadcast([P, 8, P])).then_inc(sv_done, 1)
            dve.wait_ge(dn_rows_kept, g + 1)
            gcb = by_head(two_banks(0))
            own.step(dve.tensor_tensor(stat[:, 5, 0:GROUP], stat[:, 4, 0:GROUP],
                                       gb_nat[:, GROUP * g:GROUP * (g + 1)], ALU.subtract))
            for c in range(TT):
                for b in range(GROUP):
                    r = 16 * c + GROUP * g + b
                    ins = dve.scalar_tensor_tensor(out=decay[:, c, b * P:(b + 1) * P], in0=gcb[:, b, c * P:(c + 1) * P],
                                                   scalar=gb_nat[:, r:r + 1], in1=causal[:, :],
                                                   op0=ALU.subtract, op1=ALU.add)
            ins.then_inc(dn_diff, 1)
            dve.wait_ge(dn_kk, g + 1)
            dve.wait_ge(dn_decay, g + 1)
            own.step(dve.tensor_tensor(low_t[:, :, :], small[:, 2:4, :], decay[:, :, :], ALU.mult))
            own.wait()
            dve.tensor_tensor(split_chunk(low_t[:, :, :]), split_chunk(low_t[:, :, :]), by_chunk(beta_b[:, :, :]),
                              ALU.mult).then_inc(dn_low, 1)
            dve.wait_ge(dn_qk, g + 1)
            dve.scalar_tensor_tensor(out=qk_t[:, :, :], in0=small[:, 0:2, :], scalar=DK ** -0.5, in1=decay[:, :, :],
                                     op0=ALU.mult, op1=ALU.mult).then_inc(dn_scores, 1)

            lows = low_t[:, :, :].rearrange("p c (b i) -> p (c b) i", i=P)
            off = w_off.rearrange("p (a b) -> p a b", b=P)
            dve.wait_ge(dn_low, g + 1)
            dve.tensor_tensor(off, lows, level[:, 0:1, :].to_broadcast([P, 8, P]), ALU.mult).then_inc(sv_join, 1)
            own.step(dve.scalar_tensor_tensor(out=q_dec[:, :, :], in0=qkv[:, 0:GROUP, P:], scalar=DK ** -0.5,
                                              in1=q_dec[:, :, :], op0=ALU.mult, op1=ALU.mult))
            b1 = 32 + 16 + DN_H + GROUP * g
            own.step(dve.tensor_tensor(stat[:, 6, 0:GROUP], stat[:, 6, 0:GROUP], gb_nat[:, b1:b1 + GROUP], ALU.mult))
            own.wait()

            def scaled(to, bank, factor):
                return dve.tensor_tensor(to.rearrange("p (b i) -> p b i", i=P),
                                         small[:, bank, :].rearrange("p (b i) -> p b i", i=P),
                                         factor.unsqueeze(2).to_broadcast([P, GROUP, P]), ALU.mult)

            dve.wait_ge(dn_turned, 2 * g + 1)
            for c in range(TT):
                b0 = 32 + 16 * c + DN_H + GROUP * g
                ins = scaled(v_nat[:, c, :], 2 + c, gb_nat[:, b0:b0 + GROUP])
            ins.then_inc(dn_nat, 1)
            dve.wait_ge(dn_turned, 2 * g + 2)
            scaled(k_nat[:, 0, :], 0, stat[:, 5, 0:GROUP])
            scaled(k_nat[:, 1, :], 1, stat[:, 6, 0:GROUP]).then_inc(dn_nat, 1)

            with dve.Fori(0, LEVELS) as l:
                dve.wait_ge(sv_prod, l * 2 + (14 * g + 2))
                dve.tensor_tensor(off, lows, level[:, bass.ds(l + 1, 1), :].to_broadcast([P, 8, P]),
                                  ALU.mult).then_inc(sv_join, 1)
                dve.wait_ge(sv_corr, l * 2 + (14 * g + 1))
                dve.tensor_tensor(w_x, w_x, two_banks(0), ALU.subtract).then_inc(sv_done, 1)
                dve.wait_ge(sv_corr, l * 2 + (14 * g + 2))
                dve.tensor_tensor(w_xt, w_xt, two_banks(2), ALU.subtract).then_inc(sv_done, 1)

            dve.wait_ge(dn_step, 4 * g + 3)
            dve.wait_ge(sv_join, 8 * (g + 1))
            dve.tensor_copy(st1, small[:, 2, :]).then_inc(dn_step_kept_v, 1)
            dve.wait_ge(dn_step, 4 * g + 4)
            dve.tensor_copy(vn1, small[:, 3, :]).then_inc(dn_step_kept_v, 1)
            dve.wait_ge(dn_rnorm, 2 * g + 2)
            lt = low_t[:, :, :].rearrange("p a n -> p (a n)")
            own.step(dve.scalar_tensor_tensor(out=w_x, in0=w_x, scalar=parm("dn_norm", 0), in1=lt, op0=ALU.mult,
                                              op1=ALU.mult))
            own.wait()
            own.step(dve.tensor_tensor(w_x, w_x, z_t[:, :, :].rearrange("p b t -> p (b t)"), ALU.mult))
            own.wait()
            y = slice(GROUP * g, GROUP * (g + 1))
            own.step(dve.tensor_copy(y_hi[:, y, :], by_head(w_x)))
            own.wait()
            dve.tensor_tensor(y_lo[:, y, :], by_head(w_x), y_hi[:, y, :].bitcast(F32), ALU.subtract).then_inc(y_split, 1)

        def delta_pe(pe, g):
            def each(out, lhs, rhs, start=True, stop=True):
                for b in range(GROUP):
                    c = slice(b * P, (b + 1) * P)
                    ins = pe.matmul(out[:, c], lhs[:, c], rhs[:, c], start=start and b == 0, stop=stop, skip_group_check=True)
                return ins

            pe.wait_ge(dn_square, g + 1)
            if g == 0:
                pe.wait_ge(ab_kept, 1)
            for i in range(4):
                ins = pe.matmul(small[:, i, :], ones[:, :], w_sq[:, i * CH:(i + 1) * CH], start=True, stop=True)
            ins.then_inc(dn_sumsq, 1)
            pe.wait_ge(dn_rnorm, 2 * g + 1)
            for first, src, row in ((0, g_sum, GROUP * g), (2, beta, DN_H + GROUP * g)):
                for b in range(GROUP):
                    ins = pe.matmul(by_head(two_banks(first))[:, b, :],
                                    ident[0:2 * DN_H, row + b:row + b + 1].to_broadcast([2 * DN_H, P]), src[:, :],
                                    start=b % 2 == 0, stop=True, skip_group_check=True)
            ins.then_inc(dn_rows_b, 1)
            pe.wait_ge(dn_unit, g + 1)
            pe.wait_ge(dn_rows_kept, g + 1)

            def products(bank, c, other):
                for b in range(GROUP):
                    k = qkv[:, GROUP + b, c * P:(c + 1) * P]
                    ins = pe.matmul(small[:, bank, b * P:(b + 1) * P], k, qkv[:, other + b, c * P:(c + 1) * P],
                                    start=b == 0, stop=True, skip_group_check=True)
                return ins

            for c in range(TT):
                ins = products(2 + c, c, GROUP)
            ins.then_inc(dn_kk, 1)
            pe.wait_ge(dn_diff, g + 1)
            for c in range(TT):
                ins = products(c, c, 0)
            ins.then_inc(dn_qk, 1)
            for ready, bank, src in ((dn_low, 2, 2 * GROUP), (dn_scores, 0, GROUP)):
                pe.wait_ge(ready, g + 1)
                for c in range(TT):
                    for b in range(GROUP):
                        ins = pe.transpose(small[:, bank + c, b * P:(b + 1) * P], qkv[:, src + b, c * P:(c + 1) * P],
                                           ident[:, :])
                ins.then_inc(dn_turned, 1)

            pe.wait_ge(dn_nat, 2 * (g + 1))
            chunk = [slice(c * HP, (c + 1) * HP) for c in range(TT)]
            with pe.Fori(0, LEVELS) as l:
                pe.wait_ge(sv_join, l + (8 * g + 1))
                pe.wait_ge(sv_done, l * 2 + (16 * g + 1))
                for c in range(TT):
                    each(small[:, c, :], w_off[:, chunk[c]], w_x[:, chunk[c]]).then_inc(sv_prod, 1)
                pe.wait_ge(sv_done, l * 2 + (16 * g + 2))
                for c in range(TT):
                    pe.wait_ge(sv_kept, l * 2 + (14 * g + c + 1))
                    ins = each(small[:, c, :], w_xt[:, chunk[c]], w_prod[:, chunk[c]])
                ins.then_inc(sv_corr, 1)
                for c in range(TT):
                    ins = each(small[:, 2 + c, :], w_prod[:, chunk[c]], w_xt[:, chunk[c]])
                ins.then_inc(sv_corr, 1)

            pe.wait_ge(sv_done, 16 * (g + 1))
            each(small[:, 0, :], w_xt[:, chunk[0]], v_nat[:, 0, :]).then_inc(dn_step, 1)
            each(small[:, 1, :], k_nat[:, 1, :], w_xt[:, chunk[1]]).then_inc(dn_step, 1)
            pe.wait_ge(dn_step_kept, 2 * g + 1)
            each(small[:, 2, :], k_nat[:, 0, :], u0).then_inc(dn_step, 1)
            each(small[:, 3, :], w_xt[:, chunk[1]], v_nat[:, 1, :], stop=False)
            pe.wait_ge(dn_step_kept, 2 * g + 2)
            pe.wait_ge(dn_step_kept_v, 2 * g + 1)
            each(small[:, 3, :], nw, st1, start=False).then_inc(dn_step, 1)
            pe.wait_ge(dn_step_kept_v, 2 * g + 2)
            o = by_head(two_banks(0))
            for b in range(GROUP):
                c = slice(b * P, (b + 1) * P)
                pe.matmul(o[:, b, 0:P], u0[:, c], qk_t[:, 0, c], start=b % 2 == 0, stop=True, skip_group_check=True)
                pe.matmul(o[:, b, P:], st1[:, c], q_dec[:, b, :], start=False, stop=False, skip_group_check=True)
                ins = pe.matmul(o[:, b, P:], vn1[:, c], qk_t[:, 1, c], start=False, stop=True, skip_group_check=True)
            ins.then_inc(dn_out, 1)
            pe.wait_ge(dn_out_sq, g + 1)
            for i in range(2):
                ins = pe.matmul(small[:, 2 + i, :], ones[:, :], w_xt[:, i * CH:(i + 1) * CH], start=True, stop=True)
            ins.then_inc(dn_out_rms, 1)

        def taps_act(act, taps, group, done):
            for b in range(4):
                for u in range(taps // TAP_U):
                    n = b * taps // TAP_U + u
                    if n >= 2:
                        act.wait_ge(cv_diag_used, done + (n - 1))
                    for t in range(TAP_U):
                        w = parm_at("dw", group * 4 + (KT * (TAPS - taps + u * TAP_U + t) + b))
                        ins = act.activation(tap_diag[:, n % 2, t, :], ident[:, :], ACT.Copy, scale=w)
                    ins.then_inc(cv_diag, 1)

        def taps_pe(pe, taps, group, done):
            pe.wait_ge(glu_done, group + 1)
            for b in range(4):
                for u in range(taps // TAP_U):
                    n = b * taps // TAP_U + u
                    pe.wait_ge(cv_diag, done + (n + 1))
                    for t in range(TAP_U):
                        j = TAPS - taps + u * TAP_U + t
                        ins = pe.matmul(small[:, 2 + b // 2, (b % 2) * T:(b % 2 + 1) * T], tap_diag[:, n % 2, t, :],
                                        pad30[:, b, j:j + T], start=b % 2 == 0 and u + t == 0, stop=j == TAPS - 1,
                                        skip_group_check=True)
                    ins.then_inc(cv_diag_used, 1)

        def tap_dve(dve, n, group, before):
            j, b = n // 4, n % 4
            o, u, w = cv[:, bass.ds(group * 4 + b, 1), :], pad30[:, b:b + 1, j:j + T], parm_at("dw", group * 4 + (KT * j + b))
            if j == 0:
                ins = dve.tensor_scalar(o, u, w, parm_at("dw_b", group * 4 + b), ALU.mult, ALU.add)
            else:
                dve.wait_ge(cv_tap, before + (n - 3))
                ins = dve.scalar_tensor_tensor(out=o, in0=u, scalar=w, in1=o, op0=ALU.mult, op1=ALU.add)
            ins.then_inc(cv_tap, 1)

        def taps_add(dve, group, taps, done):
            dve.wait_ge(cv_tap, taps)
            dve.wait_ge(cv_diag_used, done)
            o = cv[:, bass.ds(group * 4, 4), :]
            dve.tensor_tensor(o, o, small[:, 2:4, :].rearrange("p a n -> p (a n)").rearrange("p (b t) -> p b t", t=T),
                              ALU.add).then_inc(cv_added, 1)

        PE_STEPS = 4 * PE_TAPS // TAP_U
        PE_STEPS_LAST = 4 * PE_TAPS_LAST // TAP_U
        DVE_STEPS = 4 * (TAPS - PE_TAPS)
        DVE_STEPS_LAST = 4 * (TAPS - PE_TAPS_LAST)

        IDENT_MADE = 3
        TAPS_DN = 6 * 4 * DN_TAPS
        MERGE_L = (32, 6)
        w_in0, up0, down0, w1, w2 = w_in[0], w_up[0], w_down[0], mlp_w1_2[0], mlp_w2_2[0]

        @block.sync
        def _(sp):
            for j, group in enumerate(groups):
                r = 0
                for _, a in group:
                    sp.dma_start(rows_in[r:r + a.shape[0], j, :], a).then_inc(par_loaded, 16)
                    r += a.shape[0]
            sp.dma_start(sinks[:, :], swa_sinks.to_broadcast([P, WIN_H])).then_inc(vec_loaded, 16)
            sp.wait_ge(const_made, 1)
            sp.dma_start(dt_b[0:DN_H, :], dn_dt_bias.rearrange("a n -> n a")).then_inc(vec_loaded, 16)
            sp.dma_start(a_log[0:DN_H, :], dn_a_log.rearrange("a n -> n a")).then_inc(vec_loaded, 16)

            load_chunk(sp, spot("ab", 0), w_in0, 0, C_AB, P)
            for g in range(2):
                for m in range(4):
                    load_chunk(sp, spot("delta", 4 * g + m), w_in0, 0, m * DN_W + g * CH)
            load_chunk(sp, spot("window", 0), w_in0, 0, C_WQ)
            load_chunk(sp, spot("window", 1), w_in0, 0, C_WKV, 4 * WIN_DH)
            for m in range(3):
                load_chunk(sp, spot("stick", m), w_in0, 0, C_ST + m * CH)
            with sp.Fori(0, 4) as i:
                L = (i, *MERGE_L)
                for m in range(3):
                    load_chunk(sp, spot("merge", m, L), w_in0, 0, at(C_GATE + m * D, (i, CH)))
                for m, (w, part) in enumerate(((w_br_dn, 2), (w_br_swa, 4), (w_br_sb, 8))):
                    load_chunk(sp, spot("merge", 3 + m, L), w[0], 0, i * part * (CH // part))
            with sp.Fori(0, 2) as i:
                for m in range(2):
                    load_chunk(sp, spot("mix_out", m, (i, 16, 2)), w_o[0], 0, i * (2 * CH) + m * CH)
            for m in range(2):
                load_chunk(sp, spot("mem_kv", m), w_xkv[0], 0, m * CH)
            load_chunk(sp, spot("cross_q", 0), w_xq[0], 0, 0)
            for m in range(4):
                load_chunk(sp, spot("cross_out", m), w_xo[0], 0, m * CH)
            with sp.Fori(0, 2) as f:
                L = (f, FFN_U, FFN_C)
                with sp.Fori(0, 4) as i:
                    for m in range(2):
                        load_chunk(sp, spot("ffn_up", m, L, (i, 16, 2)), up0, 0, at(m * FF, (f, D), (i, CH)))
                with sp.Fori(0, 2) as i:
                    for m in range(2):
                        load_chunk(sp, spot("ffn_down", m, L, (i, 16, 2)), down0, f * D, at(m * CH, (i, 2 * CH)))
            with sp.Fori(0, 4) as i:
                for m in range(2):
                    load_chunk(sp, spot("conv_in", m, (i, 16, 2)), conv_w_in_2[0], 0, at(m * D, (i, CH)))
            with sp.Fori(0, 2) as i:
                for m in range(2):
                    load_chunk(sp, spot("conv_out", m, (i, 16, 2)), conv_w_out_2[0], 0, at(m * CH, (i, 2 * CH)))
            with sp.Fori(0, MLP_Q) as q:
                L = (q, MLP_U, MLP_C)
                with sp.Fori(0, 2) as i:
                    for m in range(2):
                        load_chunk(sp, spot("mlp_up", m, L, (i, 16, 2)), w1, 0, at(m * CH, (q, D), (i, 2 * CH)))
                with sp.Fori(0, 2) as i:
                    for m in range(2):
                        load_chunk(sp, spot("mlp_down", m, L, (i, 16, 2)), w2, q * D, at(m * CH, (i, 2 * CH)))
            for t in range(TT):
                sp.wait_ge(h_added, ADDED)
                sp.dma_start(out[0].rearrange("(t p) d -> t p d", p=P)[t], h[:, t, :]).then_inc(out_stored, 16)
            sp.wait_ge(out_stored, 16 * TT)

        @block.gpsimd
        def _(pool):
            made = [0]

            def then(ins):
                made[0] += 1
                ins.then_inc(const_made, 1)
                pool.wait_ge(const_made, made[0])

            def keep(t, op, base, pattern, channel, fill):
                then(pool.affine_select(out=t, in_=t, compare_op=op, fill=fill, base=base, pattern=pattern,
                                        channel_multiplier=channel))

            pool.memset(dt_b[:, :], 0.0)
            then(pool.memset(a_log[:, :], 0.0))
            then(pool.memset(ident[:, :], 0.0))
            keep(ident[:, :], ALU.not_equal, 0, [[-1, P]], 1, 1.0)
            then(pool.memset(ones[:, :], 1.0))
            then(pool.memset(twice[:, :, :], 0.0))
            keep(twice[:, :, :].rearrange("p a (r d) -> p a r d", r=2), ALU.not_equal, 0, [[-64, 2], [0, 2], [-1, 64]], 1, 1.0)
            then(pool.memset(later[:, :], 1.0))
            keep(later[:, :], ALU.is_ge, 0, [[-1, P]], 1, 0.0)
            then(pool.memset(causal[:, :], 0.0))
            keep(causal[:, :], ALU.is_ge, 0, [[1, P]], -1, -FAR)
            then(pool.memset(strict[:, :], 0.0))
            keep(strict[:, :], ALU.is_gt, 0, [[1, P]], -1, -FAR)
            then(pool.memset(level[:, :, :], 0.0))
            for l in range(LEVELS):
                half = 1 << l
                n = P // (2 * half)
                right = level[:, l, :].rearrange("p (n two r) -> p n two r", two=2, r=half)[:, :, 1, :]
                then(pool.memset(right, 1.0))
                keep(right, ALU.is_ge, 0, [[-2 * half, n], [0, half]], 1, 0.0)
                keep(right, ALU.is_ge, half - 1, [[2 * half, n], [0, half]], -1, 0.0)
            then(pool.iota(dist[:, :], pattern=[[-1, 2 * P]], base=P, channel_multiplier=1,
                           allow_small_or_imprecise_dtypes=True))
            keep(dist[:, :], ALU.is_ge, P, [[-1, 2 * P]], 1, FAR)
            pool.affine_select(out=dist[:, :], in_=dist[:, :], compare_op=ALU.is_ge, fill=FAR, base=-1,
                               pattern=[[1, 2 * P]], channel_multiplier=-1).then_inc(const_ready, 1)

            pool.wait_ge(y_split, 4)

            def load_mod(q, kt, slot):
                row = kt * P if isinstance(kt, int) else bass.ds(kt * P, P)
                src = mod_w_2[0][row if not isinstance(row, int) else slice(row, row + P), bass.ds(q * MOD_W, MOD_W)]
                pool.dma_start(mod_raw[:, slot, :], src).then_inc(mod_loaded[slot], 16)

            for j in range(2):
                pool.dma_start(mod_raw[:, j, :], mod_w_2[0][j * P:(j + 1) * P, 0:MOD_W]).then_inc(mod_loaded[j], 16)
            with pool.Fori(1, KT // 2) as v:
                for j in range(2):
                    pool.wait_ge(mod_used, v * 2 + (j - 1))
                    load_mod(0, v * 2 + j, j)
            with pool.Fori(1, MOD_G) as q:
                with pool.Fori(0, KT // 2) as v:
                    for j in range(2):
                        pool.wait_ge(mod_used, at(j - 1, (q, KT), (v, 2)))
                        load_mod(q, v * 2 + j, j)

            pool.wait_ge(ff_split, 8)
            pool.wait_ge(mod_kept, MOD_G)
            pool.dma_start(final_b[:, :], norm_final.rearrange("(a n) -> a n", a=1).to_broadcast([P, D])).then_inc(wide_loaded, 16)
            pool.dma_start(bias_b[:, :], conv_b_out_2.to_broadcast([P, D])).then_inc(wide_loaded, 16)

        @block.scalar
        def _(act):
            own = Own(act, act_own)

            def finished(s, more=0):
                act.wait_ge(unit_used, s.units(s.size))

            act.dma_start(h[:, :, :], x[0].rearrange("(t p) d -> p t d", p=P)).then_inc(x_loaded, 16)
            act.wait_ge(x_loaded, 16)
            rms_act(act, 0, h, norm_x)

            for j, group in enumerate(groups):
                n = sum(a.shape[0] for _, a in group)
                act.wait_ge(par_turned, j + 1)
                act.activation(par[:, col[group[0][0]]:col[group[0][0]] + n], small[:, j % 4, 0:n],
                               ACT.Copy).then_inc(par_kept, 1)
            act.wait_ge(par_kept, len(groups))
            act.activation(cond[:, :], parm("c", 0, KT), ACT.Silu).then_inc(cond_made, 1)

            round_units(act, spot("ab", 0), 0, 2)
            round_units(act, spot("delta", 0), 0, 2)

            act.wait_ge(eps_made, 1)
            norm_act(act, 0, norm_v, lambda kt: parm("mix", kt))

            s = spot("ab", 0)
            round_units(act, s, *ahead(s))
            act.wait_ge(const_ready, 1)
            act.wait_ge(vec_loaded, 48)
            act.activation(a_exp[:, :], a_log[:, :], ACT.Exp)
            finished(s)
            act.activation(beta[:, :], sums[0:2 * DN_H, s.pair, 0, 0:T], ACT.Sigmoid)
            act.activation(work[0:2 * DN_H, 0, 0:T], sums[0:2 * DN_H, s.pair, 0, 0:T], ACT.Identity,
                           bias=dt_b[:, 0:1]).then_inc(bank_read[s.pair], 1)
            act.wait_ge(ab_abs, 1)
            own.step(act.activation(work[0:2 * DN_H, 1, 0:T], work[0:2 * DN_H, 1, 0:T], ACT.Exp, scale=-1.0))
            own.wait()
            act.activation(work[0:2 * DN_H, 1, 0:T], work[0:2 * DN_H, 1, 0:T], ACT.Ln, bias=1.0).then_inc(ab_log, 1)

            for g in range(2):
                for m in range(4):
                    s = spot("delta", 4 * g + m)
                    if m < 3:
                        round_units(act, s, *ahead(s))
                    else:
                        round_units(act, s, SLOTS, s.size)
                        delta_silu(act, own, g)
                        round_units(act, s, s.size, s.size + SLOTS)
                    finished(s)
                    if m < 3:
                        if 3 * g + m:
                            act.wait_ge(tap_done, 4 * DN_TAPS * (3 * g + m))
                        act.activation(pad3[:, :, DN_TAPS - 1:], chunk_sums(s), ACT.Copy).then_inc(bank_read[s.pair], 1)
                    else:
                        if g:
                            act.wait_ge(y_split, g)
                        act.activation(z_t[:, :, :], chunk_sums(s), ACT.Silu).then_inc(bank_read[s.pair], 1)
                delta_act(act, own, g)

            s = spot("window", 0)
            round_units(act, s, *ahead(s))
            finished(s)
            act.wait_ge(y_split, 2)
            act.activation(win_q[:, :, :], chunk_sums(s), ACT.Copy, scale=WIN_DH ** -0.5).then_inc(bank_read[s.pair], 1)
            s = spot("window", 1)
            round_units(act, s, *ahead(s))
            finished(s)
            act.activation(win_k[:, :], sums[:, s.pair, 0, 0:T], ACT.Copy)
            act.activation(win_v[:, :, :].rearrange("p a b -> p (a b)"), sums[:, s.pair, 1, 0:T],
                           ACT.Copy).then_inc(bank_read[s.pair], 1)
            act.wait_ge(win_twice, 1)
            act.activation(win_k2[:, :, :], small[:, 0:2, 0:T], ACT.Copy).then_inc(win_twice_kept, 1)
            for n, (q, keys, to, scale) in enumerate(((1, 2 * P, st_q, ST_DH ** -0.5), (0, P, st_k, 1.0))):
                soft_act(act, n, soft_s, keys, sinks)
                s = spot("stick", n)
                round_units(act, s, *ahead(s))
                finished(s)
                act.activation(to[:, :, :], chunk_sums(s), ACT.Copy, scale=scale).then_inc(bank_read[s.pair], 1)
                soft_keep(act, keys, soft_pt, 4 * n)
                act.wait_ge(heads_out, n + 1)
                act.activation(heads_o[:, :, q * P:(q + 1) * P], small[:, 0, :].rearrange("p (a b) -> p a b", b=P),
                               ACT.Copy).then_inc(heads_kept, 1)

            s = spot("stick", 2)
            round_units(act, s, *ahead(s))
            finished(s)
            act.activation(st_v[:, :, :], sums[:, s.pair, :, :], ACT.Copy).then_inc(bank_read[s.pair], 1)
            act.wait_ge(st_masked, 1)
            own.step(act.activation(st_e[:, :, :], st_e[:, :, :], ACT.Exp, scale=-1.0))
            own.wait()
            act.activation(st_e[:, :, :], st_e[:, :, :], ACT.Ln, bias=1.0).then_inc(st_log, 1)
            act.wait_ge(st_arg, 1)
            act.activation(st_z[:, :, :], st_z[:, :, :], ACT.Exp).then_inc(st_weight, 1)
            act.wait_ge(heads_out, 3)
            act.wait_ge(y_split, 3)
            act.activation(heads_o[:, :, :], small[:, 0:2, :].rearrange("p a n -> p (a n)").rearrange("p (b t) -> p b t", t=T),
                           ACT.Copy).then_inc(heads_kept, 1)

            act.wait_ge(y_split, 4)
            with act.Fori(0, 4) as i:
                L = (i, *MERGE_L)
                for m in range(3):
                    s = spot("merge", m, L)
                    round_units(act, s, *ahead(s))
                    finished(s)
                    act.activation(gate[:, m, :, :], chunk_sums(s), ACT.Sigmoid).then_inc(bank_read[s.pair], 1)
                for m in range(3, 6):
                    s = spot("merge", m, L)
                    round_units(act, s, *ahead(s))
            act.wait_ge(unit_used, spot("mix_out", 0).unit)
            act.dma_start(mem_in[:, :, :], mem[0].rearrange("(t p) d -> p t d", p=P)).then_inc(mem_loaded, 16)
            for c in range(4):
                s = spot("mix_out", c % 2, (c // 2, 16, 2))
                round_units(act, s, *ahead(s))
                if c == 0:
                    act.wait_ge(mem_loaded, 16)
                    rms_act(act, 1, mem_in, mem_x)
                if c == 2:
                    norm_act(act, 1, mem_v, lambda kt: parm("mem", kt))

            added(act, spot("mix_out", 0, (1, 16, 2)), spot("mix_out", 1, (1, 16, 2)))
            rms_act(act, 2, h, norm_x2)
            s = spot("mem_kv", 0)
            round_units(act, s, *ahead(s))
            finished(s)
            act.activation(cr_k[:, :, :], chunk_sums(s), ACT.Copy).then_inc(bank_read[s.pair], 1)
            norm_act(act, 2, norm_v2, lambda kt: parm("xattn", kt))
            s = spot("mem_kv", 1)
            round_units(act, s, *ahead(s))
            finished(s)
            act.activation(cr_v[:, :, :], sums[:, s.pair, :, :], ACT.Copy).then_inc(bank_read[s.pair], 1)
            s = spot("cross_q", 0)
            round_units(act, s, *ahead(s))
            finished(s)
            act.activation(cr_q[:, :, :], chunk_sums(s), ACT.Copy, scale=X_DH ** -0.5).then_inc(bank_read[s.pair], 1)
            soft_act(act, 2, cr_s, T, None)
            soft_keep(act, T, cr_pt, 6)
            act.wait_ge(heads_out, 4)
            act.activation(cr_o[:, :, :], small[:, 0:2, :].rearrange("p a n -> p (a n)").rearrange("p (b t) -> p b t", t=T),
                           ACT.Copy).then_inc(heads_kept, 1)
            for m in range(4):
                s = spot("cross_out", m)
                round_units(act, s, *ahead(s))

            added(act, spot("cross_out", 2), spot("cross_out", 3))
            rms_act(act, 3, h, norm_x2)
            norm_act(act, 3, norm_v2, lambda kt: parm("ffn", kt))
            with act.Fori(0, 2) as f:
                L = (f, FFN_U, FFN_C)
                with act.Fori(0, 4) as i:
                    s = spot("ffn_up", 0, L, (i, 16, 2))
                    round_units(act, s, *ahead(s))
                    finished(s)
                    act.activation(pad2[:, :, FF_TAPS - 1:], chunk_sums(s), ACT.Copy).then_inc(bank_read[s.pair], 1)
                    s = spot("ffn_up", 1, L, (i, 16, 2))
                    round_units(act, s, *ahead(s))
                    act.wait_ge(tap_done, at(TAPS_DN + 4 * FF_TAPS, (f, 32 * FF_TAPS), (i, 8 * FF_TAPS)))
                    act.activation(ff_g[:, :, :], ff_g[:, :, :], ACT.Silu).then_inc(silu_done, 1)
                    finished(s)
                    act.activation(pad2[:, :, FF_TAPS - 1:], chunk_sums(s), ACT.Copy).then_inc(bank_read[s.pair], 1)
                with act.Fori(0, 2) as i:
                    for m in range(2):
                        s = spot("ffn_down", m, L, (i, 16, 2))
                        round_units(act, s, *ahead(s))

            L = (1, FFN_U, FFN_C)
            added(act, spot("ffn_down", 0, L, (1, 16, 2)), spot("ffn_down", 1, L, (1, 16, 2)))
            act.wait_ge(mod_kept, MOD_G)
            rms_act(act, 4, h, norm_x3)
            for n in range(2):
                wide_act(act, n)

            act.wait_ge(final_ready, TT)
            rms_act(act, 5, h, norm_x3)
            norm_act(act, 4, norm_v3, lambda kt: eff[:, kt:kt + 1], lambda kt: mod[:, kt:kt + 1])
            def values(i):
                s = spot("conv_in", 0, (i, 16, 2))
                round_units(act, s, *ahead(s))
                finished(s)
                for b in range(4):
                    ins = act.activation(cv_a[:, b, :], chunk_sums(s)[:, b, :], ACT.Identity, bias=parm_at("b_in", i * 4 + b))
                ins.then_inc(bank_read[s.pair], 1)

            def gates(i):
                s = spot("conv_in", 1, (i, 16, 2))
                round_units(act, s, *ahead(s))
                finished(s)
                for b in range(4):
                    ins = act.activation(cv_g[:, b, :], chunk_sums(s)[:, b, :], ACT.Sigmoid,
                                         bias=parm_at("b_in", i * 4 + (KT + b)))
                ins.then_inc(bank_read[s.pair], 1)

            values(0)
            gates(0)
            with act.Fori(1, 4) as i:
                act.wait_ge(glu_done, i)
                values(i)
                taps_act(act, PE_TAPS, i + (-1), i * PE_STEPS + (-PE_STEPS))
                gates(i)
            taps_act(act, PE_TAPS_LAST, 3, 3 * PE_STEPS)
            act.wait_ge(ln_sum, 1)
            act.activation(ln_m[:, 0, :], small[:, 0, 0:T], ACT.Copy, scale=1.0 / D).then_inc(ln_mean, 1)
            for j in range(4):
                act.wait_ge(ln_centred, j + 1)
                if j >= 2:
                    act.wait_ge(ln_var, j - 1)
                act.activation((cv_a, cv_g)[j % 2][:, :, :], cv[:, 4 * j:4 * j + 4, :], ACT.Square).then_inc(ln_square, 1)
            act.wait_ge(ln_var, 4)
            own.step(act.activation(ln_m[:, 1, :], small[:, 1, 0:T], ACT.Ln, scale=1.0 / D, bias=eps_col[:, 0:1]))
            own.wait()
            act.activation(ln_m[:, 1, :], ln_m[:, 1, :], ACT.Exp, scale=-0.5).then_inc(ln_rstd, 1)
            for j in range(4):
                act.wait_ge(ln_normed, j + 1)
                for b in range(4 * j, 4 * j + 4):
                    ins = act.activation(cv[:, b, :], cv[:, b, :], ACT.Silu, scale=parm("ln_g", b), bias=parm("ln_b", b))
                ins.then_inc(ln_silu, 1)
            with act.Fori(0, 2) as i:
                for m in range(2):
                    s = spot("conv_out", m, (i, 16, 2))
                    round_units(act, s, *ahead(s))

            act.wait_ge(h_added, 4)
            rms_act(act, 6, h, norm_x3)
            norm_act(act, 5, norm_v3, lambda kt: eff[:, kt:kt + 1], lambda kt: mod[:, 3 * KT + kt:3 * KT + kt + 1])

            def up(L):
                with act.Fori(0, 2) as i:
                    for m in range(2):
                        s = spot("mlp_up", m, L, (i, 16, 2))
                        round_units(act, s, *ahead(s))
                        finished(s)
                        act.activation(ml_r[:, :, :], chunk_sums(s), ACT.Relu).then_inc(bank_read[s.pair], 1)

            def down(L, i, last):
                for m in range(2):
                    s = spot("mlp_down", m, L, (i, 16, 2))
                    round_units(act, s, *ahead(s, last and m == 1))

            with act.Fori(0, MLP_Q - 1) as q:
                L = (q, MLP_U, MLP_C)
                up(L)
                with act.Fori(0, 2) as i:
                    down(L, i, False)
            L = (MLP_Q - 1, MLP_U, MLP_C)
            up(L)
            down(L, 0, False)
            down(L, 1, True)

        @block.vector
        def _(dve):
            own = Own(dve, dve_own)

            def finished(s):
                dve.wait_ge(unit_used, s.units(s.size))

            def add_sums(s, column):
                finished(s)
                c = h[:, :, column:column + CH] if isinstance(column, int) else h[:, :, bass.ds(column, CH)]
                dve.tensor_tensor(c, sums[:, s.pair, :, :], c, ALU.add).then_inc(bank_read[s.pair], 1)

            def clear_mod():
                dve.memset(mod_acc[:, :], 0.0).then_inc(mod_clear, 1)

            dve.memset(eps_col[:, :], EPS).then_inc(eps_made, 1)
            dve.wait_ge(x_loaded, 16)
            rms_dve(dve, own, 0)
            scale_rows(dve, h, norm_x)
            rest_units(dve, spot("ab", 0), 0, 2)
            rest_units(dve, spot("delta", 0), 0, 2)
            split_channels(dve, own, 0, norm_v, x_hi, x_lo)
            own.step(dve.memset(pad3[:, :, 0:DN_TAPS - 1], 0.0))

            s = spot("ab", 0)
            rest_units(dve, s, *ahead(s))
            a, e = work[0:2 * DN_H, 0, 0:T], work[0:2 * DN_H, 1, 0:T]
            dve.wait_ge(bank_read[s.pair], s.reads(1))
            dve.scalar_tensor_tensor(out=e, in0=a, scalar=-1.0, in1=a, op0=ALU.mult, op1=ALU.max).then_inc(ab_abs, 1)
            dve.wait_ge(ab_log, 1)
            own.step(dve.scalar_tensor_tensor(out=a, in0=a, scalar=0.0, in1=e, op0=ALU.max, op1=ALU.add))
            own.wait()
            own.step(dve.tensor_scalar(a, a, a_exp[:, 0:1], -1.0, ALU.mult, ALU.mult))
            own.wait()
            dve.wait_ge(const_ready, 1)
            for c in range(TT):
                dve.tensor_tensor_scan(g_sum[:, c * P:(c + 1) * P], ones[0:2 * DN_H, :], a[:, c * P:(c + 1) * P], 0.0,
                                       ALU.mult, ALU.add).then_inc(ab_sum, 1)
            dve.wait_ge(ab_turned, 1)
            dve.tensor_copy(gb_nat[:, :], small[:, 0, 0:64]).then_inc(ab_kept, 1)

            for g in range(2):
                for m in range(4):
                    s = spot("delta", 4 * g + m)
                    rest_units(dve, s, *ahead(s))
                    if m < 3:
                        dve.wait_ge(bank_read[s.pair], s.reads(1))
                        base = 4 * DN_TAPS * (3 * g + m)
                        for i in range(DN_TAPS):
                            for b in range(GROUP):
                                o, u = qkv[:, GROUP * m + b, :], pad3[:, b, i:i + T]
                                w = parm("dn_conv", 24 * i + DN_H * m + GROUP * g + b)
                                if i == 0:
                                    ins = dve.tensor_scalar(o, u, w, None, ALU.mult)
                                else:
                                    dve.wait_ge(tap_done, base + 4 * (i - 1) + b + 1)
                                    ins = dve.scalar_tensor_tensor(out=o, in0=u, scalar=w, in1=o, op0=ALU.mult, op1=ALU.add)
                                ins.then_inc(tap_done, 1)
                delta_dve(dve, own, g)

            for m in range(2):
                s = spot("window", m)
                rest_units(dve, s, *ahead(s))
            for n, (q, keys) in enumerate(((1, 2 * P), (0, P))):
                dve.wait_ge(soft_scores, n + 1)
                for b in range(WIN_H):
                    own.step(dve.scalar_tensor_tensor(out=soft_s[:, b, 0:keys], in0=dist[:, 2 * P - keys:],
                                                      scalar=-2.0 ** (-8.0 * (b + 1) / WIN_H),
                                                      in1=win_scores(b, keys),
                                                      op0=ALU.mult, op1=ALU.add))
                own.wait()
                soft_dve(dve, own, n, soft_s, keys, sinks, soft_pt)
                s = spot("stick", n)
                rest_units(dve, s, *ahead(s))
            heads_split(dve, own, 2, heads_o[:, :, :], 8)

            s = spot("stick", 2)
            rest_units(dve, s, *ahead(s))
            dve.wait_ge(st_scores, 1)
            for c in (0, 2):
                own.step(dve.tensor_tensor(st_z[:, :, c * P:(c + 1) * P], small[:, :, c * P:(c + 1) * P],
                                           strict[:, :].unsqueeze(1).to_broadcast([P, ST_H, P]), ALU.add))
            own.step(dve.tensor_copy(st_z[:, :, P:2 * P], small[:, :, P:2 * P]))
            own.wait()
            dve.scalar_tensor_tensor(out=st_e[:, :, :], in0=st_z[:, :, :], scalar=-1.0, in1=st_z[:, :, :], op0=ALU.mult,
                                     op1=ALU.max).then_inc(st_masked, 1)
            dve.wait_ge(st_log, 1)
            dve.scalar_tensor_tensor(out=st_e[:, :, :], in0=st_z[:, :, :], scalar=0.0, in1=st_e[:, :, :],
                                     op0=ALU.max, op1=ALU.add).then_inc(st_cost, 1)
            dve.wait_ge(st_summed, 1)
            dve.tensor_tensor(st_z[:, :, :], st_z[:, :, :], small[:, :, 0:3 * P], ALU.subtract).then_inc(st_arg, 1)
            heads_split(dve, own, 3, heads_o[:, :, :], 12)

            with own.loop(4, 3) as i:
                L = (i, *MERGE_L)
                clear_mod()
                kt = 0
                for m, units in enumerate((5, 5, 4, 2, 0, 0)):
                    s = spot("merge", m, L)
                    rest_units(dve, s, *ahead(s), lambda j: mod_unit(dve, kt + j, kt + j, (i, KT)), units)
                    kt += units
                    if m < 3:
                        continue
                    finished(s)
                    gs = spot("merge", m - 3, L)
                    dve.wait_ge(bank_read[gs.pair], gs.reads(1))
                    dve.tensor_tensor(gate[:, m - 3, :, :], chunk_sums(s), gate[:, m - 3, :, :],
                                      ALU.mult).then_inc(bank_read[s.pair], 1)
                    dve.wait_ge(bank_read[s.pair], s.reads(1))
                    if m > 3:
                        own.step(dve.tensor_tensor(gate[:, 0, :, :], gate[:, 0, :, :], gate[:, m - 3, :, :], ALU.add))
                        own.wait()
                own.step(dve.tensor_copy(m_hi[:, bass.ds(i * 4, 4), :], gate[:, 0, :, :]))
                own.wait()
                dve.tensor_tensor(m_lo[:, bass.ds(i * 4, 4), :], gate[:, 0, :, :],
                                  m_hi[:, bass.ds(i * 4, 4), :].bitcast(F32), ALU.subtract).then_inc(merged, 1)
                mod_keep(dve, i, i + 1)
            clear_mod()
            for c in range(4):
                s = spot("mix_out", c % 2, (c // 2, 16, 2))
                rest_units(dve, s, *ahead(s), lambda j: mod_unit(dve, 4 * KT + 4 * c + j, 4 * c + j), 4)
                add_sums(s, c * CH)
                if c == 0:
                    dve.wait_ge(mem_loaded, 16)
                    rms_dve(dve, own, 1)
                if c == 1:
                    scale_rows(dve, mem_in, mem_x)
                if c == 2:
                    split_channels(dve, own, 1, mem_v, x_hi, x_lo)
            mod_keep(dve, 4, 5)

            clear_mod()
            rms_dve(dve, own, 2)
            scale_rows(dve, h, norm_x2)
            for m, (name, c) in enumerate((("mem_kv", 0), ("mem_kv", 1), ("cross_q", 0))):
                s = spot(name, c)
                rest_units(dve, s, *ahead(s), lambda j: mod_unit(dve, 5 * KT + 5 * m + j, 5 * m + j), (5, 5, 6)[m])
                if m == 0:
                    split_channels(dve, own, 2, norm_v2, y_hi, y_lo)
            dve.wait_ge(soft_scores, 3)
            own.step(dve.tensor_copy(cr_s[:, :, :].rearrange("p a b -> p (a b)"), small[:, :, :].rearrange("p a b -> p (a b)")))
            own.wait()
            soft_dve(dve, own, 2, cr_s, T, None, cr_pt)
            heads_split(dve, own, 4, cr_o[:, :, :], 0)
            mod_keep(dve, 5, 6)
            for m in range(4):
                s = spot("cross_out", m)
                rest_units(dve, s, *ahead(s))
                add_sums(s, m * CH)

            rms_dve(dve, own, 3)
            norm_dve(dve, own, 3, h, norm_x2, norm_v2, x_hi, x_lo)
            own.step(dve.memset(pad2[:, :, 0:FF_TAPS - 1], 0.0))
            with own.loop(2, 8) as f:
                L = (f, FFN_U, FFN_C)
                clear_mod()
                with own.loop(4, 2) as i:
                    for m, to in enumerate((ff_g, ff_v)):
                        s = spot("ffn_up", m, L, (i, 16, 2))
                        rest_units(dve, s, *ahead(s), lambda j: mod_unit(dve, 6 * KT + 2 * m + j, i * 4 + (2 * m + j),
                                                                         (f, KT), (i, 4)), 2)
                        dve.wait_ge(bank_read[s.pair], s.reads(1))
                        base = TAPS_DN + 4 * FF_TAPS * m
                        for j in range(FF_TAPS):
                            for b in range(4):
                                o, u = to[:, b, :], pad2[:, b, j:j + T]
                                w = parm_at("ffn_conv", at(2 * FF // P * j + FF // P * m + b, (f, KT), (i, 4)))
                                if j == 0:
                                    ins = dve.tensor_scalar(o, u, w, None, ALU.mult)
                                else:
                                    dve.wait_ge(tap_done, at(base + 4 * (j - 1) + b + 1, (f, 32 * FF_TAPS), (i, 8 * FF_TAPS)))
                                    ins = dve.scalar_tensor_tensor(out=o, in0=u, scalar=w, in1=o, op0=ALU.mult, op1=ALU.add)
                                ins.then_inc(tap_done, 1)
                    dve.wait_ge(tap_done, at(TAPS_DN + 8 * FF_TAPS, (f, 32 * FF_TAPS), (i, 8 * FF_TAPS)))
                    dve.wait_ge(silu_done, at(1, (f, 4), (i, 1)))
                    own.step(dve.tensor_tensor(ff_v[:, :, :], ff_v[:, :, :], ff_g[:, :, :], ALU.mult))
                    own.wait()
                    own.step(dve.tensor_copy(y_hi[:, bass.ds(i * 4, 4), :], ff_v[:, :, :]))
                    own.wait()
                    dve.tensor_tensor(y_lo[:, bass.ds(i * 4, 4), :], ff_v[:, :, :],
                                      y_hi[:, bass.ds(i * 4, 4), :].bitcast(F32), ALU.subtract).then_inc(ff_split, 1)
                mod_keep(dve, at(6, (f, 1)), at(7, (f, 1)))
                with dve.Fori(0, 2) as i:
                    for m in range(2):
                        s = spot("ffn_down", m, L, (i, 16, 2))
                        rest_units(dve, s, *ahead(s))
                        add_sums(s, at(m * CH, (i, 2 * CH)))

            dve.wait_ge(mod_kept, MOD_G)
            wide_dve(dve, 0, 2)
            wide_dve(dve, 1, 5)
            rms_dve(dve, own, 4)
            dve.wait_ge(wide_loaded, 32)
            for t in range(TT):
                dve.scalar_tensor_tensor(out=h[:, t, :], in0=h[:, t, :], scalar=stat[:, 3, t:t + 1], in1=final_b[:, :],
                                         op0=ALU.mult, op1=ALU.mult).then_inc(final_ready, 1)

            dve.wait_ge(mod_kept, MOD_G)
            own.step(dve.scalar_tensor_tensor(out=eff[:, :], in0=mod[:, KT:2 * KT], scalar=1.0, in1=parm("n1", 0, KT),
                                              op0=ALU.add, op1=ALU.mult))
            dve.wait_ge(final_ready, TT)
            rms_dve(dve, own, 5)
            norm_dve(dve, own, 4, h, norm_x3, norm_v3, x_hi, x_lo)
            own.step(dve.memset(pad30[:, :, 0:TAPS - 1], 0.0))
            def glu(i):
                for m in range(2):
                    c = spot("conv_in", m, (i, 16, 2))
                    dve.wait_ge(bank_read[c.pair], c.reads(1))
                dve.tensor_tensor(pad30[:, :, TAPS - 1:], cv_a[:, :, :], cv_g[:, :, :], ALU.mult).then_inc(glu_done, 1)
                dve.wait_ge(glu_done, i + 1)

            for m in range(2):
                s = spot("conv_in", m)
                rest_units(dve, s, *ahead(s))
            glu(0)
            with dve.Fori(1, 4) as i:
                before, third = i * DVE_STEPS + (-DVE_STEPS), DVE_STEPS // 3
                s = spot("conv_in", 0, (i, 16, 2))
                rest_units(dve, s, *ahead(s), lambda n: tap_dve(dve, n, i + (-1), before), third)
                for n in range(third, DVE_STEPS - third):
                    tap_dve(dve, n, i + (-1), before)
                s = spot("conv_in", 1, (i, 16, 2))
                rest_units(dve, s, *ahead(s), lambda n: tap_dve(dve, DVE_STEPS - third + n, i + (-1), before), third)
                taps_add(dve, i + (-1), i * DVE_STEPS, i * PE_STEPS)
                glu(i)
            for n in range(DVE_STEPS_LAST):
                tap_dve(dve, n, 3, 3 * DVE_STEPS)
            taps_add(dve, 3, 3 * DVE_STEPS + DVE_STEPS_LAST, 3 * PE_STEPS + PE_STEPS_LAST)
            dve.wait_ge(ln_mean, 1)
            for j in range(4):
                c = cv[:, 4 * j:4 * j + 4, :]
                dve.tensor_tensor(c, c, ln_m[:, 0:1, :].to_broadcast([P, 4, T]), ALU.subtract).then_inc(ln_centred, 1)
            dve.wait_ge(ln_rstd, 1)
            for j in range(4):
                c = cv[:, 4 * j:4 * j + 4, :]
                dve.tensor_tensor(c, c, ln_m[:, 1:2, :].to_broadcast([P, 4, T]), ALU.mult).then_inc(ln_normed, 1)
            for j in range(4):
                c = cv[:, 4 * j:4 * j + 4, :]
                dve.wait_ge(ln_silu, j + 1)
                own.step(dve.tensor_copy(y_hi[:, 4 * j:4 * j + 4, :], c))
                own.wait()
                dve.tensor_tensor(y_lo[:, 4 * j:4 * j + 4, :], c, y_hi[:, 4 * j:4 * j + 4, :].bitcast(F32),
                                  ALU.subtract).then_inc(cv_split, 1)
            tmp = cv_a[:, :, :].rearrange("p a b -> p (a b)").rearrange("p (t n) -> p t n", n=CH)
            dve.wait_ge(diag_kept, 8)
            with own.loop(2, 2) as i:
                for m in range(2):
                    s = spot("conv_out", m, (i, 16, 2))
                    rest_units(dve, s, *ahead(s))
                    finished(s)
                    c = bass.ds(at(m * CH, (i, 2 * CH)), CH)
                    wide = (P, TT, CH)
                    dve.tensor_tensor(tmp, sums[:, s.pair, :, :], bias_b[:, c].unsqueeze(1).to_broadcast(wide),
                                      ALU.add).then_inc(bank_read[s.pair], 1)
                    dve.wait_ge(bank_read[s.pair], s.reads(1))
                    own.step(dve.tensor_tensor(tmp, tmp, gate_b[:, 0, c].unsqueeze(1).to_broadcast(wide), ALU.mult))
                    own.wait()
                    dve.tensor_tensor(h[:, :, c], h[:, :, c], tmp, ALU.add).then_inc(h_added, 1)

            own.step(dve.scalar_tensor_tensor(out=eff[:, :], in0=mod[:, 4 * KT:5 * KT], scalar=1.0, in1=parm("n2", 0, KT),
                                              op0=ALU.add, op1=ALU.mult))
            dve.wait_ge(h_added, 4)
            rms_dve(dve, own, 6)
            norm_dve(dve, own, 5, h, norm_x3, norm_v3, x_hi, x_lo)

            def up(L):
                with own.loop(2, 4) as i:
                    for m in range(2):
                        s = spot("mlp_up", m, L, (i, 16, 2))
                        rest_units(dve, s, *ahead(s))
                        dve.wait_ge(bank_read[s.pair], s.reads(1))
                        own.step(dve.tensor_tensor(ml_r[:, :, :], ml_r[:, :, :], ml_r[:, :, :], ALU.mult))
                        own.wait()
                        y = bass.ds(i * 8 + 4 * m, 4)
                        own.step(dve.tensor_copy(y_hi[:, y, :], ml_r[:, :, :]))
                        own.wait()
                        dve.tensor_tensor(y_lo[:, y, :], ml_r[:, :, :], y_hi[:, y, :].bitcast(F32),
                                          ALU.subtract).then_inc(ml_split, 1)

            def down(L, i, last):
                for m in range(2):
                    s = spot("mlp_down", m, L, (i, 16, 2))
                    rest_units(dve, s, *ahead(s, last and m == 1))
                    finished(s)
                    c = bass.ds(at(m * CH, (i, 2 * CH)), CH)
                    dve.tensor_tensor(ml_t[:, :, :], sums[:, s.pair, :, :], gate_b[:, 1, c].unsqueeze(1).to_broadcast((P, TT, CH)),
                                      ALU.mult).then_inc(bank_read[s.pair], 1)
                    dve.wait_ge(bank_read[s.pair], s.reads(1))
                    dve.tensor_tensor(h[:, :, c], h[:, :, c], ml_t[:, :, :], ALU.add).then_inc(h_added, 1)

            with own.loop(MLP_Q - 1, 8) as q:
                L = (q, MLP_U, MLP_C)
                up(L)
                with dve.Fori(0, 2) as i:
                    down(L, i, False)
            L = (MLP_Q - 1, MLP_U, MLP_C)
            up(L)
            down(L, 0, False)
            down(L, 1, True)

        @block.tensor
        def _(pe):
            pe.wait_ge(const_made, IDENT_MADE)
            pe.wait_ge(par_loaded, 16 * n_par_loads)
            for j, group in enumerate(groups):
                n = sum(a.shape[0] for _, a in group)
                if j >= 4:
                    pe.wait_ge(par_kept, j - 3)
                pe.transpose(small[:, j % 4, 0:n], rows_in[0:n, j, :], ident[0:n, 0:n]).then_inc(par_turned, 1)
            pe.wait_ge(par_kept, len(groups))

            norm_pe(pe, 0, norm_x, spot("ab", 0), x_hi, x_lo, True, P)
            pe.wait_ge(const_ready, 1)
            pe.wait_ge(ab_sum, TT)
            for a, rows16 in enumerate((g_sum, beta)):
                for c in range(TT):
                    ins = pe.transpose(small[:, 0, 32 * a + 16 * c:32 * a + 16 * (c + 1)], rows16[:, c * P:(c + 1) * P],
                                       ident[0:2 * DN_H, 0:2 * DN_H])
            ins.then_inc(ab_turned, 1)
            for g in range(2):
                for m in range(4):
                    multiply(pe, spot("delta", 4 * g + m), x_hi, x_lo, True)
                delta_pe(pe, g)

            multiply(pe, spot("window", 0), x_hi, x_lo, True)
            s = spot("window", 1)
            multiply_kv(pe, s)
            pe.wait_ge(bank_read[s.pair], s.reads(1))
            s0 = spot("window", 0)
            pe.wait_ge(bank_read[s0.pair], s0.reads(1))
            for kv in range(2):
                ins = pe.matmul(small[:, kv, 0:T], twice[:, kv, :], win_k[:, :], start=True, stop=True)
            ins.then_inc(win_twice, 1)
            pe.wait_ge(win_twice_kept, 1)
            for n, (q, keys) in enumerate(((1, 2 * P), (0, P))):
                if n:
                    pe.wait_ge(heads_kept, n)
                for b in range(WIN_H):
                    hf = slice(64 * (b % 2), 64 * (b % 2) + 64)
                    ins = pe.matmul(win_scores(b, keys),
                                    win_q[hf, b // 2, q * P:(q + 1) * P], win_k2[hf, b // 4, 0:keys], start=True,
                                    stop=True)
                ins.then_inc(soft_scores, 1)
                multiply(pe, spot("stick", n), x_hi, x_lo, True)
                soft_pe(pe, n, soft_s, keys)
                tiles = keys // P
                pe.wait_ge(soft_kept, (4, 6)[n])
                for b in range(WIN_H):
                    kv = b // 4
                    for k in range(tiles):
                        ins = pe.matmul(small[64 * (b % 2):64 * (b % 2) + 64, 0, (b // 2) * P:(b // 2 + 1) * P],
                                        win_v[:, k, kv * WIN_DH:(kv + 1) * WIN_DH], soft_pt[:, b * tiles + k, :],
                                        start=k == 0, stop=k == tiles - 1, skip_group_check=True)
                ins.then_inc(heads_out, 1)

            multiply(pe, spot("stick", 2), x_hi, x_lo, False)
            for m in range(3):
                s = spot("stick", m)
                pe.wait_ge(bank_read[s.pair], s.reads(1))
            pe.wait_ge(heads_kept, 2)
            for b in range(ST_H):
                pe.matmul(small[:, b, 0:T], st_k[:, b, 0:P], st_q[:, b, :], start=True, stop=True, skip_group_check=True)
                ins = pe.matmul(small[:, b, T:T + P], st_k[:, b, P:T], st_q[:, b, P:T], start=True, stop=True,
                                skip_group_check=True)
            ins.then_inc(st_scores, 1)
            pe.wait_ge(st_cost, 1)
            for b in range(ST_H):
                pe.matmul(small[:, b, 0:3 * P], later[:, :], st_e[:, b, :], start=True, stop=False, skip_group_check=True)
                ins = pe.matmul(small[:, b, P:T], ones[:, :], st_e[:, b, T:T + P], start=False, stop=True,
                                skip_group_check=True)
            ins.then_inc(st_summed, 1)
            pe.wait_ge(st_weight, 1)
            for b in range(ST_H):
                o = small[:, b // 2, (b % 2) * T:(b % 2 + 1) * T]
                pe.matmul(o, st_v[:, 0, b * P:(b + 1) * P], st_z[:, b, 0:T], start=True, stop=False, skip_group_check=True)
                ins = pe.matmul(o[:, P:T], st_v[:, 1, b * P:(b + 1) * P], st_z[:, b, T:T + P], start=False, stop=True,
                                skip_group_check=True)
            ins.then_inc(heads_out, 1)

            pe.wait_ge(y_split, 4)
            with pe.Fori(0, 4) as i:
                L = (i, *MERGE_L)
                for m in range(3):
                    multiply(pe, spot("merge", m, L), x_hi, x_lo, True)
                for m, k0 in ((3, 0), (4, 8), (5, 12)):
                    multiply(pe, spot("merge", m, L), y_hi, y_lo, True, k0=k0)
                mod_sum(pe, at(KT, (i, KT)))
            for c in range(4):
                multiply(pe, spot("mix_out", c % 2, (c // 2, 16, 2)), m_hi, m_lo, False,
                         before=None if c else lambda tile, end: pe.wait_ge(merged, tile // 4 + 1))
                if c == 2:
                    pe.wait_ge(mod_kept, 4)
                    pe.wait_ge(norm_scaled, 2 * TT)
                    turn_rows(pe, 1, mem_x, 0, NG)

            pe.wait_ge(norm_split, 2 * NG)
            mod_sum(pe, 5 * KT)
            multiply(pe, spot("mem_kv", 0), x_hi, x_lo, True)
            pe.wait_ge(mod_kept, 5)
            pe.wait_ge(norm_scaled, 3 * TT)
            turn_rows(pe, 2, norm_x2, 0, NG)
            multiply(pe, spot("mem_kv", 1), x_hi, x_lo, False)
            pe.wait_ge(norm_split, 3 * NG)
            multiply(pe, spot("cross_q", 0), y_hi, y_lo, True)
            for s in (spot("mem_kv", 0), spot("mem_kv", 1), spot("cross_q", 0)):
                pe.wait_ge(bank_read[s.pair], s.reads(1))
            for b in range(X_H):
                for q in range(TT):
                    ins = pe.matmul(small[:, b, q * T:(q + 1) * T], cr_q[:, b, q * P:(q + 1) * P], cr_k[:, b, :],
                                    start=True, stop=True, skip_group_check=True)
            ins.then_inc(soft_scores, 1)
            soft_pe(pe, 2, cr_s, T)
            pe.wait_ge(soft_kept, 10)
            for b in range(X_H):
                for q in range(TT):
                    o = small[:, b // 2, (b % 2) * T + q * P:(b % 2) * T + (q + 1) * P]
                    for k in range(TT):
                        ins = pe.matmul(o, cr_v[:, k, b * P:(b + 1) * P], cr_pt[:, (b * TT + q) * TT + k, :],
                                        start=k == 0, stop=k == 1, skip_group_check=True)
            ins.then_inc(heads_out, 1)
            mod_sum(pe, 6 * KT)
            pe.wait_ge(y_split, 5)
            for m in range(4):
                multiply(pe, spot("cross_out", m), y_hi, y_lo, False)

            def half(f, first):
                L = (f, FFN_U, FFN_C)
                with pe.Fori(first, 4) as i:
                    for m in range(2):
                        multiply(pe, spot("ffn_up", m, L, (i, 16, 2)), x_hi, x_lo, True)
                mod_sum(pe, at(7 * KT, (f, KT)))
                with pe.Fori(0, 2) as i:
                    multiply(pe, spot("ffn_down", 0, L, (i, 16, 2)), y_hi, y_lo, False,
                             before=lambda tile, end: pe.wait_ge(ff_split, at(tile // 4 + 1, (f, 4))))
                    multiply(pe, spot("ffn_down", 1, L, (i, 16, 2)), y_hi, y_lo, False)

            norm_pe(pe, 3, norm_x2, spot("ffn_up", 0), x_hi, x_lo, True)
            multiply(pe, spot("ffn_up", 1), x_hi, x_lo, True)
            half(0, 1)
            half(1, 0)

            pe.wait_ge(mod_kept, MOD_G)
            for n in range(2):
                wide_pe(pe, n)
            pe.wait_ge(diag_kept, 8)
            norm_pe(pe, 4, norm_x3, spot("conv_in", 0), x_hi, x_lo, True)
            multiply(pe, spot("conv_in", 1), x_hi, x_lo, True)
            with pe.Fori(1, 4) as i:
                multiply(pe, spot("conv_in", 0, (i, 16, 2)), x_hi, x_lo, True)
                taps_pe(pe, PE_TAPS, i + (-1), i * PE_STEPS + (-PE_STEPS))
                multiply(pe, spot("conv_in", 1, (i, 16, 2)), x_hi, x_lo, True)
            taps_pe(pe, PE_TAPS_LAST, 3, 3 * PE_STEPS)
            for kt in range(KT):
                if kt % 12 == 0:
                    pe.wait_ge(cv_added, 3 + kt // 12)
                ins = pe.matmul(small[:, 0, 0:T], ones[:, :], cv[:, kt, :], start=kt == 0, stop=kt == KT - 1)
            ins.then_inc(ln_sum, 1)
            for j in range(4):
                pe.wait_ge(ln_square, j + 1)
                for b in range(4):
                    ins = pe.matmul(small[:, 1, 0:T], ones[:, :], (cv_a, cv_g)[j % 2][:, b, :],
                                    start=j == 0 and b == 0, stop=j == 3 and b == 3)
                ins.then_inc(ln_var, 1)
            multiply(pe, spot("conv_out", 0), y_hi, y_lo, False, before=lambda tile, end: pe.wait_ge(cv_split, tile // 4 + 1))
            multiply(pe, spot("conv_out", 1), y_hi, y_lo, False)
            for m in range(2):
                multiply(pe, spot("conv_out", m, (1, 16, 2)), y_hi, y_lo, False)

            def up(L, i):
                for m in range(2):
                    multiply(pe, spot("mlp_up", m, L, (i, 16, 2)), x_hi, x_lo, True)

            def down(L, q):
                with pe.Fori(0, 2) as i:
                    multiply(pe, spot("mlp_down", 0, L, (i, 16, 2)), y_hi, y_lo, False,
                             before=lambda tile, end: pe.wait_ge(ml_split, at(tile // 4 + 1, (q, 4))))
                    multiply(pe, spot("mlp_down", 1, L, (i, 16, 2)), y_hi, y_lo, False)

            norm_pe(pe, 5, norm_x3, spot("mlp_up", 0), x_hi, x_lo, True)
            multiply(pe, spot("mlp_up", 1), x_hi, x_lo, True)
            L = (0, MLP_U, MLP_C)
            up(L, 1)
            down(L, 0)
            with pe.Fori(1, MLP_Q) as q:
                L = (q, MLP_U, MLP_C)
                with pe.Fori(0, 2) as i:
                    up(L, i)
                down(L, q)


_INS = ['x', 'mem', 'w_in', 'dn_conv', 'dn_a_log', 'dn_dt_bias', 'dn_norm', 'norm_mix', 'swa_sinks', 'w_br_dn',
        'w_br_swa', 'w_br_sb', 'w_o', 'norm_xattn', 'norm_mem', 'w_xq', 'w_xkv', 'w_xo', 'norm_ffn', 'w_up',
        'ffn_conv', 'w_down', 'norm_final', 'c_2', 'norm1_g_2', 'norm2_g_2', 'mod_w_2', 'mod_b_2', 'mlp_w1_2',
        'mlp_w2_2', 'conv_w_in_2', 'conv_b_in_2', 'conv_dw_w_2', 'conv_dw_b_2', 'conv_ln_g_2', 'conv_ln_b_2',
        'conv_w_out_2', 'conv_b_out_2']


def kernel(**inputs):
    import numpy as _np
    import concourse.bacc as _bacc
    from concourse.bass_utils import run_bass_kernel_spmd as _run

    nc = _bacc.Bacc("TRN2", target_bir_lowering=False, num_devices=1)
    arrays, args = {}, []
    for name in _INS:
        a = _np.ascontiguousarray(inputs[name])
        arrays[f"in_{name}_dram"] = a
        args.append(nc.dram_tensor(f"in_{name}_dram", a.shape, mybir.dt.from_np(a.dtype), kind="ExternalInput").ap())
    out = nc.dram_tensor("out_dram", (1, T, D), F32, kind="ExternalOutput").ap()
    build_program(nc, *args, out)
    r = _run(nc, [arrays], core_ids=[0])
    return r.results[0]["out_dram"]
```
